# Optimizing a Trainium2 kernel written in Bass

```python
import jax, jax.numpy as jnp
from jax import lax
import numpy as np
import math

D_MODEL = 1024
BATCH = 1
SEQ = 512
DEPTH = 1

D_MIX = D_MODEL
A_WIDTH = D_MIX // 4
A_GROUPS = 4
A_GROUP_DIM = A_WIDTH // A_GROUPS
A_CHUNK = 128
B_WIDTH = D_MIX // 4
B_EXPAND = 64
B_HEADS = B_WIDTH // B_EXPAND
B_KDIM = B_EXPAND
B_VDIM = B_WIDTH // B_HEADS
B_FDIM = B_HEADS * B_KDIM
B_CHUNK = 128
C_WIDTH = D_MIX - A_WIDTH - B_WIDTH
C_HEAD_DIM = 64
C_HEADS = C_WIDTH // C_HEAD_DIM
C_BLOCK = 128
COL_WIDTHS = (A_WIDTH, A_WIDTH, A_WIDTH,
              B_FDIM, B_FDIM, B_WIDTH, B_WIDTH,
              C_WIDTH, C_WIDTH, C_WIDTH, C_WIDTH, C_HEADS)
D_IN = 3 * A_WIDTH + 2 * B_FDIM + 2 * B_WIDTH + 4 * C_WIDTH + C_HEADS
NORM_EPS = 1e-6
F_FLOOR = 1e-30


def _rmsnorm(x, g):
    xf = x.astype(jnp.float32)
    y = xf * lax.rsqrt(jnp.mean(xf * xf, axis=-1, keepdims=True) + NORM_EPS)
    return (y * g.astype(jnp.float32)).astype(x.dtype)

def _split_cols(proj):
    offsets = []
    acc = 0
    for w in COL_WIDTHS[:-1]:
        acc += w
        offsets.append(acc)
    return jnp.split(proj, offsets, axis=-1)

def _gmlp_mixer(u, v, ln_g, ln_b, w_s, b_s):
    bsz, seq, _ = u.shape
    nc = seq // A_CHUNK
    u = jax.nn.gelu(u)
    v = jax.nn.gelu(v).reshape(bsz, nc, A_CHUNK, A_GROUPS, A_GROUP_DIM)
    vf = v.astype(jnp.float32)
    mu = jnp.mean(vf, axis=-1, keepdims=True)
    var = jnp.mean(jnp.square(vf - mu), axis=-1, keepdims=True)
    vn = (vf - mu) * lax.rsqrt(var + NORM_EPS) * ln_g.astype(jnp.float32) + ln_b.astype(jnp.float32)
    causal = jnp.tril(jnp.ones((A_CHUNK, A_CHUNK), dtype=bool))
    w = jnp.where(causal[None], w_s.astype(jnp.float32), 0.0)
    mixed = jnp.einsum('gts,bnsgc->bntgc', w, vn)
    mixed = mixed + jnp.transpose(b_s.astype(jnp.float32))[None, None, :, :, None]
    return u * mixed.reshape(bsz, seq, A_WIDTH).astype(u.dtype)

def _hgrn2_mixer(q, f_logit, i, lb, onorm_g):
    bsz, seq, _ = q.shape
    nc = seq // B_CHUNK
    qf = jax.nn.silu(q.astype(jnp.float32)) * (B_KDIM ** -0.5)
    z = f_logit.astype(jnp.float32)
    f = lb + (1.0 - lb) * jax.nn.sigmoid(z)
    log_f = jnp.log(jnp.maximum(f, F_FLOOR))
    kf = (1.0 - lb) * jax.nn.sigmoid(-z)
    vf = i.astype(jnp.float32)

    def to_chunks(t, d):
        return t.reshape(bsz, nc, B_CHUNK, B_HEADS, d).transpose(1, 0, 3, 2, 4)

    qc, kc, gc = to_chunks(qf, B_KDIM), to_chunks(kf, B_KDIM), to_chunks(log_f, B_KDIM)
    vc = to_chunks(vf, B_VDIM)
    causal = jnp.tril(jnp.ones((B_CHUNK, B_CHUNK), dtype=bool))[None, None, :, :, None]

    def step(state, inp):
        qx, kx, vx, gx = inp
        b = jnp.cumsum(gx, axis=2)
        o_inter = jnp.einsum('bhtk,bhkv->bhtv', qx * jnp.exp(b), state)
        diff = b[:, :, :, None, :] - b[:, :, None, :, :]
        decay = jnp.exp(jnp.where(causal, diff, -jnp.inf))
        scores = jnp.einsum('bhtk,bhsk,bhtsk->bhts', qx, kx, decay)
        o_intra = jnp.einsum('bhts,bhsv->bhtv', scores, vx)
        b_last = b[:, :, -1:, :]
        new_state = (jnp.exp(b_last[:, :, 0, :])[..., None] * state
                     + jnp.einsum('bhsk,bhsv->bhkv', kx * jnp.exp(b_last - b), vx))
        return new_state, o_inter + o_intra

    state0 = jnp.zeros((bsz, B_HEADS, B_KDIM, B_VDIM), jnp.float32)
    _, ys = lax.scan(step, state0, (qc, kc, vc, gc))
    o = ys.transpose(1, 0, 3, 2, 4).reshape(bsz, seq, B_HEADS, B_VDIM)
    o = o * lax.rsqrt(jnp.mean(o * o, axis=-1, keepdims=True) + NORM_EPS) * onorm_g.astype(jnp.float32)
    return o.reshape(bsz, seq, B_WIDTH).astype(q.dtype)

def _fox_mixer(q, k, v, f_logit, b_f):
    bsz, seq, _ = q.shape

    def heads(t):
        return t.reshape(bsz, seq, C_HEADS, C_HEAD_DIM).transpose(0, 2, 1, 3)

    qh, kh, vh = heads(q), heads(k), heads(v)
    log_f = jax.nn.log_sigmoid(f_logit.astype(jnp.float32) + b_f.astype(jnp.float32))
    c = jnp.cumsum(jnp.transpose(log_f, (0, 2, 1)), axis=-1)
    scale = C_HEAD_DIM ** -0.5
    diag_mask = jnp.tril(jnp.ones((C_BLOCK, C_BLOCK), dtype=bool))
    outs = []
    for blk in range(seq // C_BLOCK):
        q0 = blk * C_BLOCK
        q1 = q0 + C_BLOCK
        s = jnp.einsum('bhqd,bhkd->bhqk', qh[:, :, q0:q1], kh[:, :, :q1]).astype(jnp.float32) * scale
        s = s + c[:, :, q0:q1, None] - c[:, :, None, :q1]
        mask = jnp.concatenate([jnp.ones((C_BLOCK, q0), dtype=bool), diag_mask], axis=1)
        s = jnp.where(mask[None, None], s, -jnp.inf)
        p = jax.nn.softmax(s, axis=-1)
        outs.append(jnp.einsum('bhqk,bhkd->bhqd', p.astype(vh.dtype), vh[:, :, :q1]))
    o = jnp.concatenate(outs, axis=2)
    return o.transpose(0, 2, 1, 3).reshape(bsz, seq, C_WIDTH)

def first_inputs(seed: int = 0) -> dict:
    key = jax.random.key(seed)
    ks = jax.random.split(key, 13)
    f32 = jnp.float32
    x = jax.random.normal(ks[0], (BATCH, SEQ, D_MODEL), f32)
    norm_g = 1.0 + 0.05 * jax.random.normal(ks[1], (DEPTH, D_MODEL), f32)
    w_in = jax.random.normal(ks[2], (DEPTH, D_MODEL, D_IN), f32) * D_MODEL ** -0.5
    w_out = jax.random.normal(ks[3], (DEPTH, D_MIX, D_MODEL), f32) * (D_MIX ** -0.5) * (2 * DEPTH) ** -0.5
    gmlp_ln_g = 1.0 + 0.05 * jax.random.normal(ks[4], (DEPTH, A_GROUPS, A_GROUP_DIM), f32)
    gmlp_ln_b = 0.02 * jax.random.normal(ks[5], (DEPTH, A_GROUPS, A_GROUP_DIM), f32)
    gmlp_w_s = jax.random.normal(ks[6], (DEPTH, A_GROUPS, A_CHUNK, A_CHUNK), f32) * A_CHUNK ** -0.5
    gmlp_b_s = 1.0 + 0.1 * jax.random.normal(ks[7], (DEPTH, A_GROUPS, A_CHUNK), f32)
    hgrn_lb = 0.1 * jax.random.normal(ks[8], (DEPTH, B_FDIM), f32)
    hgrn_onorm_g = 1.0 + 0.05 * jax.random.normal(ks[9], (DEPTH, B_VDIM), f32)
    fox_b_f = jax.random.uniform(ks[10], (DEPTH, C_HEADS), f32, 0.0, 3.0)
    final_norm_g = 1.0 + 0.05 * jax.random.normal(ks[11], (D_MODEL,), f32)
    return {"x": x, "norm_g": norm_g, "w_in": w_in, "w_out": w_out,
            "gmlp_ln_g": gmlp_ln_g, "gmlp_ln_b": gmlp_ln_b, "gmlp_w_s": gmlp_w_s,
            "gmlp_b_s": gmlp_b_s, "hgrn_lb": hgrn_lb, "hgrn_onorm_g": hgrn_onorm_g,
            "fox_b_f": fox_b_f, "final_norm_g": final_norm_g}

def first_block(x, norm_g, w_in, w_out, gmlp_ln_g, gmlp_ln_b, gmlp_w_s, gmlp_b_s,
              hgrn_lb, hgrn_onorm_g, fox_b_f, final_norm_g):
    p = jax.nn.softmax(hgrn_lb.astype(jnp.float32), axis=0)
    lb_all = jnp.clip(jnp.cumsum(p, axis=0) - p[0:1], 0.0, 1.0 - 1e-6)
    for layer in range(DEPTH):
        h = _rmsnorm(x, norm_g[layer])
        proj = jnp.einsum('bsd,de->bse', h, w_in[layer])
        (a_u, a_v, a_z, b_q, b_fl, b_i, b_z,
         c_q, c_k, c_v, c_z, c_fl) = _split_cols(proj)
        y_a = _gmlp_mixer(a_u, a_v, gmlp_ln_g[layer], gmlp_ln_b[layer],
                          gmlp_w_s[layer], gmlp_b_s[layer]) * jax.nn.silu(a_z)
        y_b = _hgrn2_mixer(b_q, b_fl, b_i, lb_all[layer], hgrn_onorm_g[layer]) * jax.nn.silu(b_z)
        y_c = _fox_mixer(c_q, c_k, c_v, c_fl, fox_b_f[layer]) * jax.nn.silu(c_z)
        y = jnp.concatenate([y_a, y_b, y_c], axis=-1)
        x = x + jnp.einsum('bse,ed->bsd', y, w_out[layer])
    return _rmsnorm(x, final_norm_g)


DEPTH_2 = 2

N_MIXERS = 2
N_LAYERS_A = (DEPTH_2 + 1) // 2
N_LAYERS_B = DEPTH_2 // 2
D_FF = 2752
FFN_HALF = 0.5
ROPE_THETA = 500000.0
ROT_FRAC = 4
Q_BLOCK = 128
EPS = 1e-6
N_MOD = 9

A_HEADS = 16
A_HEAD_DIM = 64
A_KV_DIM = 64
IDX_HEADS = 8
IDX_DIM = 64
TOPK_MAX = 256
A_Q = A_HEADS * A_HEAD_DIM
A_IN = A_Q + 2 * A_KV_DIM + IDX_HEADS * IDX_DIM + IDX_DIM + IDX_HEADS

B_HEADS_2 = 8
B_HEAD_DIM = 64
B_V_DIM = 2 * B_HEAD_DIM
B_QK = 2 * B_HEADS_2 * B_HEAD_DIM
B_IN = 2 * B_QK + B_HEADS_2 * B_V_DIM


def rmsnorm(x, g):
    xf = x.astype(jnp.float32)
    y = xf * lax.rsqrt(jnp.mean(xf * xf, axis=-1, keepdims=True) + EPS)
    return (y * g.astype(jnp.float32)).astype(x.dtype)

def modulate(h, shift, scale):
    return h * (1.0 + scale[:, None, :]) + shift[:, None, :]

def swiglu(h, w_gate, w_up, w_down):
    return (jax.nn.silu(h @ w_gate) * (h @ w_up)) @ w_down

def rope_tables(positions, head_dim):
    rot = head_dim // ROT_FRAC
    inv = ROPE_THETA ** (-jnp.arange(0, rot, 2, dtype=jnp.float32) / rot)
    ang = positions.astype(jnp.float32)[..., None] * inv
    return jnp.cos(ang), jnp.sin(ang)

def apply_rope(x, cos, sin):
    half = cos.shape[-1]
    rot = 2 * half
    shp = cos.shape[:2] + (1,) * (x.ndim - 3) + (half,)
    cos = cos.reshape(shp)
    sin = sin.reshape(shp)
    x1 = x[..., :half].astype(jnp.float32)
    x2 = x[..., half:rot].astype(jnp.float32)
    xr = jnp.concatenate([x1 * cos - x2 * sin, x2 * cos + x1 * sin], axis=-1)
    return jnp.concatenate([xr.astype(x.dtype), x[..., rot:]], axis=-1)

def dsa_mixer(h, w_in, w_out, cos, sin):
    B, S, _ = h.shape
    top_k = min(TOPK_MAX, S // 4)
    proj = h @ w_in
    o1 = A_Q
    o2 = o1 + A_KV_DIM
    o3 = o2 + A_KV_DIM
    o4 = o3 + IDX_HEADS * IDX_DIM
    o5 = o4 + IDX_DIM
    q = apply_rope(proj[..., :o1].reshape(B, S, A_HEADS, A_HEAD_DIM), cos, sin)
    k = apply_rope(proj[..., o1:o2], cos, sin)
    v = proj[..., o2:o3]
    qi = apply_rope(proj[..., o3:o4].reshape(B, S, IDX_HEADS, IDX_DIM), cos, sin)
    ki = apply_rope(proj[..., o4:o5], cos, sin)
    wi = proj[..., o5:].astype(jnp.float32) * (IDX_HEADS ** -0.5 * IDX_DIM ** -0.5)
    ki32 = ki.astype(jnp.float32)
    key_pos = jnp.arange(S)
    scale = A_HEAD_DIM ** -0.5
    gather = jax.vmap(lambda arr, ids: arr[ids])

    def block(i):
        start = i * Q_BLOCK
        t = start + jnp.arange(Q_BLOCK)
        q_b = lax.dynamic_slice_in_dim(q, start, Q_BLOCK, axis=1)
        qi_b = lax.dynamic_slice_in_dim(qi, start, Q_BLOCK, axis=1)
        wi_b = lax.dynamic_slice_in_dim(wi, start, Q_BLOCK, axis=1)
        logits = jnp.einsum('bthd,bsd->bths', qi_b.astype(jnp.float32), ki32)
        score = jnp.einsum('bth,bths->bts', wi_b, jax.nn.relu(logits))
        causal = key_pos[None, :] <= t[:, None]
        score = jnp.where(causal[None], score, -jnp.inf)
        _, idx = lax.top_k(score, top_k)
        k_sel = gather(k, idx).astype(jnp.float32)
        v_sel = gather(v, idx).astype(jnp.float32)
        s = jnp.einsum('bthd,btkd->bhtk', q_b.astype(jnp.float32), k_sel) * scale
        valid = idx <= t[None, :, None]
        s = jnp.where(valid[:, None], s, -jnp.inf)
        p = jax.nn.softmax(s, axis=-1)
        o = jnp.einsum('bhtk,btkd->bthd', p, v_sel)
        return o.reshape(B, Q_BLOCK, A_HEADS * A_KV_DIM).astype(h.dtype)

    out = lax.map(block, jnp.arange(S // Q_BLOCK))
    out = jnp.transpose(out, (1, 0, 2, 3)).reshape(B, S, A_HEADS * A_KV_DIM)
    return out @ w_out

def diff_mixer(h, w_in, w_out, lam, subln_g, cos, sin, layer_idx):
    B, S, _ = h.shape
    lam_init = 0.8 - 0.6 * math.exp(-0.3 * layer_idx)
    proj = h @ w_in
    q = apply_rope(proj[..., :B_QK].reshape(B, S, 2, B_HEADS_2, B_HEAD_DIM), cos, sin)
    k = apply_rope(proj[..., B_QK:2 * B_QK].reshape(B, S, 2, B_HEADS_2, B_HEAD_DIM), cos, sin)
    v = proj[..., 2 * B_QK:].reshape(B, S, B_HEADS_2, B_V_DIM)
    lam32 = lam.astype(jnp.float32)
    lam_val = (jnp.exp(jnp.sum(lam32[0] * lam32[1])) - jnp.exp(jnp.sum(lam32[2] * lam32[3]))
               + lam_init)
    k32 = k.astype(jnp.float32)
    v32 = v.astype(jnp.float32)
    key_pos = jnp.arange(S)
    scale = B_HEAD_DIM ** -0.5

    def block(i):
        start = i * Q_BLOCK
        t = start + jnp.arange(Q_BLOCK)
        q_b = lax.dynamic_slice_in_dim(q, start, Q_BLOCK, axis=1).astype(jnp.float32)
        s = jnp.einsum('btchd,bschd->bchts', q_b, k32) * scale
        causal = key_pos[None, :] <= t[:, None]
        s = jnp.where(causal, s, -jnp.inf)
        p = jax.nn.softmax(s, axis=-1)
        a = p[:, 0] - lam_val * p[:, 1]
        o = jnp.einsum('bhts,bshe->bthe', a, v32)
        o = rmsnorm(o, subln_g) * (1.0 - lam_init)
        return o.reshape(B, Q_BLOCK, B_HEADS_2 * B_V_DIM).astype(h.dtype)

    out = lax.map(block, jnp.arange(S // Q_BLOCK))
    out = jnp.transpose(out, (1, 0, 2, 3)).reshape(B, S, B_HEADS_2 * B_V_DIM)
    return out @ w_out

def second_inputs(seed: int = 0) -> dict:
    key = jax.random.key(seed)
    ks = jax.random.split(key, 18)
    f32 = jnp.float32

    def nrm(k, shape, fan_in, scale=1.0):
        return jax.random.normal(k, shape, f32) * (scale * fan_in ** -0.5)

    x = jax.random.normal(ks[0], (BATCH, SEQ, D_MODEL), f32)
    c = jax.random.normal(ks[1], (BATCH, D_MODEL), f32)
    offsets = jax.random.randint(ks[2], (BATCH, 1), 0, 1024, dtype=jnp.int32)
    positions = offsets + jnp.arange(SEQ, dtype=jnp.int32)[None, :]
    return {
        "x": x,
        "c": c,
        "positions": positions,
        "ada_w": nrm(ks[3], (DEPTH_2, D_MODEL, N_MOD * D_MODEL), D_MODEL, 0.5),
        "ada_b": 0.02 * jax.random.normal(ks[4], (DEPTH_2, N_MOD * D_MODEL), f32),
        "pre_norm": 1.0 + 0.05 * jax.random.normal(ks[5], (DEPTH_2, 3, D_MODEL), f32),
        "post_norm": 1.0 + 0.05 * jax.random.normal(ks[6], (DEPTH_2, 3, D_MODEL), f32),
        "ffn_w_gate": nrm(ks[7], (DEPTH_2, 2, D_MODEL, D_FF), D_MODEL),
        "ffn_w_up": nrm(ks[8], (DEPTH_2, 2, D_MODEL, D_FF), D_MODEL),
        "ffn_w_down": nrm(ks[9], (DEPTH_2, 2, D_FF, D_MODEL), D_FF),
        "dsa_w_in": nrm(ks[10], (N_LAYERS_A, D_MODEL, A_IN), D_MODEL),
        "dsa_w_out": nrm(ks[11], (N_LAYERS_A, A_HEADS * A_KV_DIM, D_MODEL), A_HEADS * A_KV_DIM),
        "diff_w_in": nrm(ks[12], (N_LAYERS_B, D_MODEL, B_IN), D_MODEL),
        "diff_w_out": nrm(ks[13], (N_LAYERS_B, B_HEADS_2 * B_V_DIM, D_MODEL), B_HEADS_2 * B_V_DIM),
        "diff_lambda": 0.1 * jax.random.normal(ks[14], (N_LAYERS_B, 4, B_HEAD_DIM), f32),
        "diff_subln": 1.0 + 0.05 * jax.random.normal(ks[15], (N_LAYERS_B, B_V_DIM), f32),
    }

def second_block(x, c, positions, ada_w, ada_b, pre_norm, post_norm, ffn_w_gate, ffn_w_up,
              ffn_w_down, dsa_w_in, dsa_w_out, diff_w_in, diff_w_out, diff_lambda, diff_subln):
    cos, sin = rope_tables(positions, A_HEAD_DIM)
    cond = jax.nn.silu(c)
    for i in range(DEPTH_2):
        mod = cond @ ada_w[i] + ada_b[i]
        sh0, sc0, g0, sh1, sc1, g1, sh2, sc2, g2 = jnp.split(mod, N_MOD, axis=-1)
        h = modulate(rmsnorm(x, pre_norm[i, 0]), sh0, sc0)
        y = swiglu(h, ffn_w_gate[i, 0], ffn_w_up[i, 0], ffn_w_down[i, 0])
        x = x + FFN_HALF * g0[:, None, :] * rmsnorm(y, post_norm[i, 0])
        h = modulate(rmsnorm(x, pre_norm[i, 1]), sh1, sc1)
        j = i // N_MIXERS
        if i % N_MIXERS == 0:
            y = dsa_mixer(h, dsa_w_in[j], dsa_w_out[j], cos, sin)
        else:
            y = diff_mixer(h, diff_w_in[j], diff_w_out[j], diff_lambda[j], diff_subln[j],
                           cos, sin, i)
        x = x + g1[:, None, :] * rmsnorm(y, post_norm[i, 1])
        h = modulate(rmsnorm(x, pre_norm[i, 2]), sh2, sc2)
        y = swiglu(h, ffn_w_gate[i, 1], ffn_w_up[i, 1], ffn_w_down[i, 1])
        x = x + FFN_HALF * g2[:, None, :] * rmsnorm(y, post_norm[i, 2])
    return x


def setup_inputs(seed=0):
    out = dict(first_inputs(seed))
    for name, value in second_inputs(seed + 1).items():
        if name != "x":
            out[name + "_2"] = value
    return out


def reference(
    x, norm_g, w_in, w_out, gmlp_ln_g, gmlp_ln_b, gmlp_w_s, gmlp_b_s, hgrn_lb, hgrn_onorm_g,
    fox_b_f, final_norm_g, c_2, positions_2, ada_w_2, ada_b_2, pre_norm_2, post_norm_2,
    ffn_w_gate_2, ffn_w_up_2, ffn_w_down_2, dsa_w_in_2, dsa_w_out_2, diff_w_in_2, diff_w_out_2,
    diff_lambda_2, diff_subln_2,
):
    x = first_block(
        x, norm_g, w_in, w_out, gmlp_ln_g, gmlp_ln_b, gmlp_w_s, gmlp_b_s, hgrn_lb, hgrn_onorm_g,
        fox_b_f, final_norm_g,
    )
    return second_block(
        x, c_2, positions_2, ada_w_2, ada_b_2, pre_norm_2, post_norm_2, ffn_w_gate_2,
        ffn_w_up_2, ffn_w_down_2, dsa_w_in_2, dsa_w_out_2, diff_w_in_2, diff_w_out_2,
        diff_lambda_2, diff_subln_2,
    )


_drawn_inputs = setup_inputs


def setup_inputs(seed=0):
    import zlib

    import numpy as np

    out = dict(_drawn_inputs(seed))
    spreads = {}
    factors = {'gmlp_ln_g': 6.423,
     'gmlp_ln_b': 28.315,
     'gmlp_b_s': 3.071,
     'hgrn_onorm_g': 3.442,
     'diff_lambda_2': 8.0,
     'diff_subln_2': 33.191}
    for name, (base, spread) in spreads.items():
        noise = np.random.default_rng([zlib.crc32(name.encode()), seed]).standard_normal(out[name].shape)
        drawn = base * np.exp(spread * noise) if base else spread * noise
        out[name] = __import__('jax').numpy.asarray(drawn.astype(out[name].dtype))
    for name, factor in factors.items():
        out[name] = (out[name] * factor).astype(out[name].dtype)
    return out
```

```python
from contextlib import ExitStack

import numpy as np

import concourse.bass as bass
from concourse import mybir

F32 = mybir.dt.float32
F32R = mybir.dt.float32r
BF16 = mybir.dt.bfloat16
U8 = mybir.dt.uint8
I32 = mybir.dt.int32
ALU = mybir.AluOpType
ACT = mybir.ActivationFunctionType
AX = mybir.AxisListType.X
ds = bass.ds

P = 128
SEQ = 512
D = 1024
KT = D // P
NT = SEQ // P
F_FF = 2752
FT = -(-F_FF // P)
FH = FT // 2
N_LAYERS = 2
MOD_TILES = 9 * D // P
HD = 64
EPS = 1e-6
F_FLOOR = 1e-30
NEG = -1.0e30
TAKEN = -3.0e38
TOPK = min(256, SEQ // 4)
N_RAW = 4
N_SPLIT = 2
N_BANKS = 4
ROPE_THETA, ROT_FRAC = 500000.0, 4
LAM_INIT = 0.8 - 0.6 * float(np.exp(-0.3 * 1))

IN_KINDS = (["gelu"] * 2 + ["gelu_tok"] * 2 + ["silu"] * 2
            + ["silu"] * 2 + ["copy"] * 2 + ["tok"] * 2 + ["silu"] * 2
            + ["copy"] * 8 + ["tok"] * 4 + ["silu"] * 4 + ["copy"])
DSA_KINDS = ["rope"] * 8 + ["rope"] + ["tok"] + ["rope"] * 4 + ["rope"]
DIFF_KINDS = ["rope"] * 16 + ["tok"] * 8

STAGE_UNITS = [("in", len(IN_KINDS)), ("out", KT),
               ("ffn0", 2 * FT + 2 * KT), ("dsa", len(DSA_KINDS)), ("dsa_out", KT), ("ffn1", 2 * FT + 2 * KT),
               ("ffn2", 2 * FT + 2 * KT), ("diff", len(DIFF_KINDS)), ("diff_out", KT), ("ffn3", 2 * FT + 2 * KT)]
STAGE_OUTS = [len(IN_KINDS), KT, 2 * FT + KT, len(DSA_KINDS), KT, 2 * FT + KT,
              2 * FT + KT, len(DIFF_KINDS), KT, 2 * FT + KT]
STAGES = [name for name, _ in STAGE_UNITS]
UNIT_BASE = {n: sum(c for _, c in STAGE_UNITS[:i]) for i, n in enumerate(STAGES)}
OUT_BASE = {n: sum(STAGE_OUTS[:i]) for i, n in enumerate(STAGES)}
FILL = {n: i for i, n in enumerate(STAGES)}
N_UNITS = sum(c for _, c in STAGE_UNITS)

SUBS = ["ffn0", "dsa", "ffn1", "ffn2", "diff", "ffn3"]
PRE = {s: 2 + 2 * i for i, s in enumerate(SUBS)}
POST = {s: 3 + 2 * i for i, s in enumerate(SUBS)}

COL = {}
_at = 0
for _name, _n in (("norm_g", KT), ("final_g", KT), ("pre", 6 * KT), ("post", 6 * KT), ("ada_b", 2 * MOD_TILES),
                  ("onorm", 1), ("subln", 1), ("lb", 2), ("inv_freq", 1), ("sign", 1), ("fox_b", 1)):
    COL[_name] = _at
    _at += _n
N_COLS = _at


def bank_plan():
    uses, plan = [0] * N_BANKS, {}
    for name, n in STAGE_UNITS:
        if name.startswith("ffn"):
            plan[name, "up"] = list(uses)
            uses = [u + 2 * FT // N_BANKS for u in uses]
            plan[name, "down"] = list(uses)
            uses = [u + (KT // 2 if b < 2 else 0) for b, u in enumerate(uses)]
        else:
            plan[name, "all"] = list(uses)
            for j in range(n):
                uses[j % N_BANKS] += 1
    return plan


BANK_USES = bank_plan()
TOK = {"in": 0, "fox_out": 8, "dsa": 12, "dsa_out": 13, "diff": 21, "diff_out": 29}


class Chain:

    def __init__(self, eng, sem):
        self.eng, self.sem, self.n, self.per, self.it = eng, sem, 0, 0, None

    def link(self, ins):
        ins.then_inc(self.sem, 1)
        self.n += 1
        self.eng.wait_ge(self.sem, self.n if self.it is None else self.it * self.per + self.n)

    def body(self, it, per):
        self.it, self.per, self.start = it, per, self.n

    def leave(self, count):
        assert self.n - self.start == self.per, (self.n - self.start, self.per)
        self.it = None
        self.n = self.start + self.per * count


def build(nc, A, out, last="ffn3"):
    ctx = ExitStack()
    with ctx:
        place = {"at": 16512}

        def sb(name, shape, dt=F32, at=None):
            size = int(np.prod(shape[1:])) * mybir.dt.size(dt)
            if at is None:
                at = place["at"]
                place["at"] = at + -(-size // 32) * 32
            return nc.alloc_sbuf_tensor_at(name, shape, dt, offset=at)

        def sem(name):
            return ctx.enter_context(nc.semaphore(name))

        run = STAGES[:STAGES.index(last) + 1]
        n_units = UNIT_BASE[last] + dict(STAGE_UNITS)[last]

        x = sb("x", [P, KT, SEQ])
        H_AT = place["at"]
        h_hi = sb("h_hi", [P, KT, SEQ], F32R)
        h_lo = sb("h_lo", [P, KT, SEQ], F32R)
        y = sb("y", [P, KT, SEQ], at=H_AT)
        raw = [sb(f"raw{i}", [P, FH * P]) for i in range(N_RAW)]
        w_hi = [sb(f"w_hi{i}", [P, FH * P], F32R) for i in range(N_SPLIT)]
        w_lo = [sb(f"w_lo{i}", [P, FH * P], F32R) for i in range(N_SPLIT)]
        ada = [sb(f"ada{i}", [P, D]) for i in range(2)]
        cond = sb("cond", [P, D])
        sq = [sb(f"sq{i}", [P, SEQ]) for i in range(2)]
        acc = sb("acc", [P, SEQ])
        rstd = sb("rstd", [P, SEQ])
        t = [sb(f"t{i}", [P, SEQ]) for i in range(2)]
        cols = sb("cols", [P, N_COLS])
        mod_raw = sb("mod_raw", [P, 2 * MOD_TILES])
        gain = sb("gain", [P, 6 * KT])
        coef = sb("coef", [P, 6 * KT])
        ident = sb("ident", [P, P])
        ones = sb("ones", [P, P])
        ident_bf = sb("ident_bf", [P, P], BF16)
        causal_bf = sb("causal_bf", [P, P], BF16)
        eps_col = sb("eps_col", [P, 1])
        lam_col = sb("lam_col", [P, 4])
        BIG = place["at"]

        def big(name, at, shape, dt=F32):
            return sb(name, shape, dt, at=BIG + 4 * at)

        a_hi = big("a_hi", 0, [P, FT, SEQ], F32R)
        a_lo = big("a_lo", FT * SEQ, [P, FT, SEQ], F32R)

        au = big("au", 0, [P, 2, SEQ])
        av = big("av", 1024, [P, NT, 256])
        az = big("az", 2048, [P, 2, SEQ])
        bq = big("bq", 3072, [P, 2, SEQ])
        bf = big("bf", 4096, [P, 2, SEQ])
        bi = big("bi", 5120, [P, NT, 256])
        bz = big("bz", 6144, [P, 2, SEQ])
        cq = big("cq", 7168, [P, 4, SEQ])
        ck = big("ck", 9216, [P, 4, SEQ])
        cv = big("cv", 11264, [P, NT, 512])
        cz = big("cz", 13312, [P, 4, SEQ])
        cf = big("cf", 15360, [P, SEQ])
        ws = big("ws", 15872, [P, 4, P])
        bs_bc = big("bs_bc", 16384, [P, 2, P])
        ln_g = big("ln_g", 16640, [P, 256])
        ln_b = big("ln_b", 16896, [P, 256])
        st = big("st", 17152, [P, 4, 16])
        level = big("level", 17216, [P, 8, P], U8)
        level_raw = big("level_raw", 21056, [P, 8, P])
        keep = big("keep", 17472, [P, SEQ])[:, :]
        bk = big("bk", 17984, [P, 2, SEQ])
        bb = big("bb", 19008, [P, 2, SEQ])
        bt = big("bt", 20032, [P, 2, SEQ])
        bx = big("bx", 21056, [P, 2, SEQ])
        state = big("state", 22080, [P, 3, 2, HD])
        bcol = big("bcol", 22464, [P, 64])
        sc = big("sc", 0, [P, 4, SEQ])
        kh_tok = big("kh_tok", 2048, [P, NT, 256])
        nc_row = big("nc_row", 0, [P, 8, SEQ])
        block1 = dict(q=cq, k=ck, v=cv, P=big("fP", 4096, [P, 4, SEQ]), PT=big("fPT", 17984, [P, 2, SEQ]),
                      otok=big("fotok", 19008, [P, NT, 512]), qs=big("fqs", 21056, [P, 1, SEQ]), ks=big("fks", 6144, [P, 1, SEQ]),
                      st=big("fst", 21568, [P, 3, 16]), ot=big("fot", 21696, [P, P]))

        y_mix = big("y_mix", 0, [P, KT, SEQ])
        dq = big("dq", 0, [P, 8, SEQ])
        dk = big("dk", 4096, [P, SEQ])
        dv = big("dv", 4608, [P, NT, P])
        dqi = big("dqi", 5120, [P, 4, SEQ])
        dki = big("dki", 7168, [P, SEQ])
        dcos = big("dcos", 7680, [P, SEQ])
        dsin = big("dsin", 8192, [P, SEQ])
        dshuf = [big(f"dshuf{i}", 8704 + 512 * i, [P, SEQ]) for i in range(2)]
        rel = [big(f"rel{i}", 9728 + 512 * i, [P, SEQ]) for i in range(2)]
        score = [big(f"score{i}", 10752 + 512 * i, [P, SEQ]) for i in range(2)]
        top8 = big("top8", 11776, [P, 2, 8])
        wi = big("wi", 11840, [P, NT, 8])
        mask = big("mask", 12288, [P, NT, SEQ], BF16)
        dsa = dict(q=dq, k=dk, v=dv, P=big("dP", 13312, [P, 4, SEQ]), PT=big("dPT", 15360, [P, 2, SEQ]),
                   otok=big("dotok", 16384, [P, NT, D]), qs=big("dqs", 20480, [P, 1, SEQ]),
                   st=big("dst", 20992, [P, 3, 16]), ot=big("dot", 21120, [P, P]))

        fq = big("fq", 0, [P, 8, SEQ])
        fk = big("fk", 4096, [P, 8, SEQ])
        fv = big("fv", 8192, [P, NT, D])
        fcos = big("fcos", 12288, [P, SEQ])
        fsin = big("fsin", 12800, [P, SEQ])
        fshuf = [big(f"fshuf{i}", 13312 + 512 * i, [P, SEQ]) for i in range(2)]
        lam_in = big("lam_in", 14336, [P, 4, HD])
        sq_o = big("sq_o", 0, [P, NT, D])
        st_o = big("st_o", 4096, [P, 32])
        diff = dict(q=fq, k=fk, v=fv, P=big("gP", 15360, [P, 4, SEQ]), PT=big("gPT", 17408, [P, 2, SEQ]),
                    otok=big("gotok", 18432, [P, NT, D]), qs=big("gqs", 13312, [P, 2, SEQ]), ks=big("gks", 12288, [P, 2, SEQ]),
                    st=big("gst", 14656, [P, 3, 16]), ot=big("got", 14720, [P, P]))

        assert BIG + 2 * 4 * FT * SEQ <= 229344, BIG + 2 * 4 * FT * SEQ

        bank = [ctx.enter_context(nc.psum_tensor(f"bank{i}", [P, SEQ], F32)) for i in range(8)]

        raw_landed = [sem(f"raw_landed{i}") for i in range(N_RAW)]
        ada_landed = [sem(f"ada_landed{i}") for i in range(2)]
        hi_ready, lo_ready = sem("hi_ready"), sem("lo_ready")
        unit_done = sem("unit_done")
        bank_free = [sem(f"bank_free{i}") for i in range(N_BANKS)]
        ada_used = sem("ada_used")
        const_landed, x_landed, c_landed = sem("const_landed"), sem("x_landed"), sem("c_landed")
        b1_landed = sem("b1_landed")
        cond_ready, const_ready = sem("cond_ready"), sem("const_ready")
        sq_ready, sums_done, ss_ready, sqrt_done, rstd_ready = (
            sem("sq_ready"), sem("sums_done"), sem("ss_ready"), sem("sqrt_done"), sem("rstd_ready"))
        t_ready, hh_ready, hl_ready = sem("t_ready"), sem("hh_ready"), sem("hl_ready")
        u_ready, x_pool, x_dve = sem("u_ready"), sem("x_pool"), sem("x_dve")
        ahi_ready, alo_ready = sem("ahi_ready"), sem("alo_ready")
        tok_T, tok_done = sem("tok_T"), sem("tok_done")
        dve_step = sem("dve_step")
        out_landed = sem("out_landed")

        block = ctx.enter_context(nc.Block())

        def read_of(stage, j, it=0):
            if not stage.startswith("ffn"):
                b = j % N_BANKS
                uses = BANK_USES[stage, "all"][b] + j // N_BANKS
            elif j < 2 * FT:
                b = j % N_BANKS
                uses = BANK_USES[stage, "up"][b] + j // N_BANKS
            else:
                b = (j - 2 * FT) % 4 // 2
                uses = BANK_USES[stage, "down"][b] + (j - 2 * FT) // 4
            return bank_free[b], uses + 1 + it

        def in_dst(j):
            for buf, lo_, hi_ in ((au, 0, 2), (az, 4, 6), (bq, 6, 8), (bf, 8, 10), (bz, 12, 14), (cq, 14, 18),
                                  (ck, 18, 22), (cz, 26, 30)):
                if lo_ <= j < hi_:
                    return buf[:, j - lo_, :]
            return cf[:, :]

        def tok_dst(stage, j):
            if stage == "dsa":
                return dv[:, :, :]
            if stage == "diff":
                return fv[:, :, (j - 16) * P:(j - 15) * P]
            for buf, lo_, hi_ in ((av, 2, 4), (bi, 10, 12), (cv, 22, 26)):
                if lo_ <= j < hi_:
                    return buf[:, :, (j - lo_) * P:(j - lo_ + 1) * P]

        def rope_dst(stage, j):
            if stage == "diff":
                return fq[:, j, :] if j < 8 else fk[:, j - 8, :]
            return dq[:, j, :] if j < 8 else dk[:, :] if j == 8 else dki[:, :] if j == 14 else dqi[:, j - 10, :]

        def y_of(sub):
            return y if sub.startswith("ffn") else y_mix

        def ffn_no(stage):
            return int(stage[3])

        def mod_col(i, seg, d):
            at = i // 3 * MOD_TILES + (3 * (i % 3) + seg) * KT + d
            return mod_raw[:, at:at + 1]

        def shift_col(i, d):
            return mod_col(i, 0, d)

        FOX_MAPS = DSA_MAPS = [(half, 0, qb) for half in range(2) for qb in range(NT)]
        DIFF_MAPS = [(half, comp, qb) for half in range(2) for qb in range(NT) for comp in range(2)]
        TOK_DONE = {"in": 0, "dsa": 8, "diff": 9}

        def raw_width(stage, j):
            return FH * P if stage.startswith("ffn") and j >= 2 * FT else D

        def unit_stage(g):
            for s in reversed(STAGES):
                if g >= UNIT_BASE[s]:
                    return s

        def width_of(g):
            s = unit_stage(g)
            return raw_width(s, g - UNIT_BASE[s])

        names = ("qs_ready", "s_ready", "nm_ready", "p_ready", "tr_ready", "pt_act", "pt_dve", "o_ready", "o_read",
                 "otok_done")
        att = {k: {n: sem(f"{k}_{n}") for n in names} for k in ("fox", "dsa", "diff")}
        rope = {k: {n: sem(f"{k}_{n}") for n in ("pos_landed", "angle", "table", "done")} for k in ("dsa", "diff")}
        fox_c_ready, fox_c_landed = sem("fox_c_ready"), sem("fox_c_landed")
        b1 = {n: sem(f"b1_{n}") for n in (
            "ws", "var", "std", "vn", "mixed", "lb", "lb_exp", "exps", "f", "ln", "b", "e_in", "e_out", "kh", "kh_T",
            "kh_tok", "kv", "state", "x", "levels", "copied", "sc", "o", "osq", "oss", "ostd", "c_in", "c_out",
            "bd")}
        ix = {n: sem(f"ix_{n}") for n in ("logit", "relu", "read", "mask")}
        lam_landed, lam_sum, lam_exp = sem("lam_landed"), sem("lam_sum"), sem("lam_exp")
        sub_sq, sub_sum, sub_std = sem("sub_sq"), sem("sub_sum"), sem("sub_std")
        has = lambda s: s in run
        if run[-1] in SUBS or run[-1] in ("dsa_out", "diff_out"):
            subs_run = sum(1 for s in SUBS if (s if s.startswith("ffn") else s + "_out") in run)
            fin_ready = (x_pool, 8 * subs_run)
        else:
            fin_ready = (x_dve, 8)

        def ada_of(stage, j):
            n0 = MOD_TILES
            if stage == "in":
                return list(range(2 * j, 2 * j + 2))
            if stage == "out":
                a = 2 * len(IN_KINDS) + 2 * j
                return list(range(a, min(a + 2, n0)))
            if stage == "ffn0":
                return [n0 + j]
            if stage == "ffn1" and j < 2 * MOD_TILES - n0 - (2 * FT + 2 * KT):
                return [n0 + 2 * FT + 2 * KT + j]
            return []

        ADA_FFN1 = (MOD_TILES - (2 * FT + 2 * KT)) // 4
        assert MOD_TILES - (2 * FT + 2 * KT) == 4 * ADA_FFN1

        def loops(stage):
            up, down = 2 * FT // 4, 2 * KT // 4
            if stage == "ffn0":
                return [(0, up, 1, "up"), (2 * FT, down, 1, "down")]
            if stage == "ffn1":
                return [(0, ADA_FFN1, 1, "up"), (4 * ADA_FFN1, up - ADA_FFN1, 0, "up"), (2 * FT, down, 0, "down")]
            return [(0, up, 0, "up"), (2 * FT, down, 0, "down")]

        def bodies(eng, count, body, chain=None, per=0):
            with eng.Fori(0, count - 1) as it:
                if chain:
                    chain.body(it, per)
                body(it)
            if chain:
                chain.leave(count - 1)
            body(count - 1)

        def ada_index(stage, first, j, it):
            base = MOD_TILES if stage == "ffn0" else MOD_TILES + 2 * FT + 2 * KT
            return base + first + j + 4 * it

        @block.sync
        def _(sp):
            sp.dma_start(x[:, :, :], A["x"].rearrange("(k p) s -> p k s", p=P)).then_inc(x_landed, 16)
            sp.dma_start(cols[:, :], A["cols"]).then_inc(const_landed, 16)
            sp.dma_start(ident[:, :], A["ident"]).then_inc(const_landed, 16)
            sp.dma_start(t[0][:, 0:P], A["causal"]).then_inc(const_landed, 16)
            sp.dma_start(cond[:, :], A["c"].partition_broadcast(P)).then_inc(c_landed, 16)

            def load_unit(stage, j, it=0):
                g = UNIT_BASE[stage] + j
                slot, w = g % N_RAW, raw_width(stage, j)
                if g >= N_RAW:
                    sp.wait_ge(lo_ready, g - N_RAW + 1 + 4 * it)
                if stage.startswith("ffn"):
                    n = int(stage[3])
                    if j < 2 * FT:
                        src = A["ffn_up"][n, ds(j + 4 * it, 1)]
                    else:
                        src = A["ffn_down"][n, ds(j - 2 * FT + 4 * it, 1)]
                    src = src.rearrange("a p n -> (a p) n")
                else:
                    src = A["w_" + stage][j]
                sp.dma_start(raw[slot][:, 0:w], src).then_inc(raw_landed[slot], 16)

            for stage in run:
                if stage == "in":
                    for j in range(len(IN_KINDS)):
                        load_unit(stage, j)
                        if j == 2:
                            b1 = [(ws[:, :, :], A["ws"]), (level_raw[:, :, :], A["level"]), (keep, A["keep"]),
                                  (ln_g[:, :], A["ln_g"].partition_broadcast(P)),
                                  (ln_b[:, :], A["ln_b"].partition_broadcast(P))]
                            for g in range(4):
                                b1.append((bs_bc[g % 2 * HD:g % 2 * HD + HD, g // 2, :],
                                           A["bs"][g].partition_broadcast(HD)))
                            for dst, src in b1:
                                sp.dma_start(dst, src).then_inc(b1_landed, 16)
                elif stage.startswith("ffn"):
                    for first, count, _ada, _part in loops(stage):
                        with sp.Fori(0, count) as it:
                            for j in range(4):
                                load_unit(stage, first + j, it)
                else:
                    for j in range(dict(STAGE_UNITS)[stage]):
                        load_unit(stage, j)

            sp.wait_ge(fin_ready[0], fin_ready[1])
            sp.dma_start(out.rearrange("(k p) s -> p k s", p=P), x[:, :, :]).then_inc(out_landed, 16)
            sp.wait_ge(out_landed, 16)


        @block.scalar
        def _(act):
            def hi(g, w, it=0):
                act.wait_ge(raw_landed[g % N_RAW], 16 * (g // N_RAW + 1) + 16 * it)
                if g >= N_SPLIT:
                    act.wait_ge(unit_done, g - N_SPLIT + 1 + 4 * it)
                act.activation(w_hi[g % N_SPLIT][:, 0:w], raw[g % N_RAW][:, 0:w], ACT.Copy).then_inc(hi_ready, 1)

            def hi_ahead(stage, j, it=0):
                g = UNIT_BASE[stage] + j + N_SPLIT
                if not isinstance(it, int):
                    hi(g, raw_width(stage, j), it)
                elif g + 4 * it < n_units:
                    hi(g, width_of(g + 4 * it), it)

            def square(n, d, src):
                need = 9 * n + (d if d >= 2 else 0)
                if need:
                    act.wait_ge(sums_done, need)
                act.activation(sq[d % 2][:, :], src, ACT.Square).then_inc(sq_ready, 1)

            def std(n):
                act.wait_ge(ss_ready, n + 1)
                act.activation(rstd[:, :], bank[6][:, :], ACT.Sqrt, bias=eps_col[:, 0:1],
                               scale=1.0 / D).then_inc(sqrt_done, 1)

            def fill_hi(stage, d, bias=None):
                if d == 0:
                    act.wait_ge(unit_done, UNIT_BASE[stage])
                act.wait_ge(t_ready, 8 * FILL[stage] + d + 1)
                if bias is None:
                    ins = act.activation(h_hi[:, d, :], t[d % 2][:, :], ACT.Copy)
                else:
                    ins = act.activation(h_hi[:, d, :], t[d % 2][:, :], ACT.Identity, bias=bias)
                ins.then_inc(hh_ready, 1)

            def squares_of_x(n, ready, base):
                for d in range(KT):
                    act.wait_ge(ready, base + d + 1)
                    square(n, d, x[:, d, :])

            def pre(stage):
                i = SUBS.index(stage)
                if i == 0:
                    squares_of_x(PRE[stage], x_dve, 0)
                else:
                    squares_of_x(PRE[stage], x_pool, 8 * (i - 1))
                std(PRE[stage])
                for d in range(KT):
                    fill_hi(stage, d, shift_col(i, d))

            def y_square(sub, stage, j, d):
                act.wait_ge(*read_of(stage, j))
                square(POST[sub], d, y_mix[:, d, :])

            def ffn(stage):
                pre(stage)
                for first, count, _ada, part in loops(stage):
                    def up(it):
                        for f in range(2):
                            j = first + 2 * f
                            hi_ahead(stage, j, it)
                            act.wait_ge(unit_done, UNIT_BASE[stage] + j + 1 + 4 * it)
                            act.activation(sq[f][:, :], bank[2 * f][:, :], ACT.Silu).then_inc(bank_free[2 * f], 1)
                            hi_ahead(stage, j + 1, it)
                            act.wait_ge(*read_of(stage, j + 1, it))
                            act.activation(a_hi[:, ds(first // 2 + f + 2 * it, 1), :].rearrange("p a n -> p (a n)"),
                                           t[f][:, :], ACT.Copy).then_inc(ahi_ready, 1)

                    def down(it):
                        for d in range(2):
                            j = first + 2 * d
                            hi_ahead(stage, j, it)
                            hi_ahead(stage, j + 1, it)
                            act.wait_ge(*read_of(stage, j + 1, it))
                            act.wait_ge(sums_done, 9 * POST[stage] + d + 2 * it)
                            act.activation(sq[d][:, :], y[:, ds(2 * it + d, 1), :].rearrange("p a n -> p (a n)"),
                                           ACT.Square).then_inc(sq_ready, 1)
                    bodies(act, count, up if part == "up" else down)
                std(POST[stage])

            def evac_unit(stage, j, func, dst):
                act.wait_ge(unit_done, UNIT_BASE[stage] + j + 1)
                return act.activation(dst, bank[j % N_BANKS][:, :], func)

            def attend(k, cfg, maps, rounds):
                s = att[k]
                B = len(maps)
                with act.Fori(0, rounds) as it:
                    def exp(u):
                        qb = maps[u][2]
                        w = (qb + 1) * P
                        act.wait_ge(s["nm_ready"], B * it + u + 1)
                        if u >= 4:
                            act.wait_ge(s["tr_ready"], B * it + u - 3)
                        act.activation(cfg["P"][:, u % 4, 0:w], bank[u % 4][:, 0:w], ACT.Exp,
                                       bias=cfg["st"][:, 0, u:u + 1],
                                       accum_out=cfg["st"][:, 1, u:u + 1]).then_inc(s["p_ready"], 1)
                    exp(0)
                    exp(1)
                    for u in range(B):
                        if u % 2 == 0:
                            w = (maps[u][2] + 1) * P
                            act.wait_ge(s["tr_ready"], B * it + u + 1)
                            if u >= 2:
                                act.wait_ge(s["o_ready"], B * it + u - 1)
                            act.activation(cfg["PT"][:, 0, 0:w], bank[4][:, 0:w], ACT.Copy).then_inc(s["pt_act"], 1)
                        if u + 2 < B:
                            exp(u + 2)

            def block1_mixers():
                act.wait_ge(b1["var"], 1)
                act.activation(st[:, 3, :], st[:, 2, :], ACT.Sqrt, bias=eps_col[:, 0:1],
                               scale=1.0 / HD).then_inc(b1["std"], 1)
                for d in (0, 1):
                    fill_hi("out", d)
                act.wait_ge(b1["lb"], 1)
                act.activation(bcol[:, 2:4], bcol[:, 0:2], ACT.Exp).then_inc(b1["lb_exp"], 1)
                act.activation(bk[:, :, :], bf[:, :, :], ACT.Exp).then_inc(b1["exps"], 1)
                act.activation(bt[:, :, :], bf[:, :, :], ACT.Exp, scale=-1.0).then_inc(b1["exps"], 1)
                act.wait_ge(b1["f"], 1)
                act.activation(bf[:, :, :], bf[:, :, :], ACT.Ln).then_inc(b1["ln"], 1)
                act.wait_ge(b1["b"], 1)
                act.activation(bt[:, :, :], bb[:, :, :], ACT.Exp).then_inc(b1["e_out"], 1)
                act.activation(bcol[:, 8:16].rearrange("p (a n) -> p a n", a=2),
                               bb[:, :, :].rearrange("p a (n s) -> p a n s", s=P)[:, :, :, P - 1],
                               ACT.Exp).then_inc(b1["e_out"], 1)
                for i in range(8):
                    act.wait_ge(b1["e_in"], i + 1)
                    buf = bx if i % 2 == 0 else bf
                    act.activation(buf[:, :, :], buf[:, :, :], ACT.Exp).then_inc(b1["e_out"], 1)
                for a in range(2):
                    act.wait_ge(b1["o"], a + 1)
                    act.activation(bx[:, a, :], bank[4 + a][:, :], ACT.Square).then_inc(b1["osq"], 1)
                for a in range(2):
                    act.wait_ge(b1["oss"], a + 1)
                    act.activation(bt[:, a, :], bank[6 + a][:, :], ACT.Sqrt, bias=eps_col[:, 0:1],
                                   scale=1.0 / HD).then_inc(b1["ostd"], 1)
                for d in (2, 3):
                    fill_hi("out", d)
                act.wait_ge(b1["c_in"], 1)
                act.activation(bt[0:8, 0, :], bt[0:8, 0, :], ACT.Exp).then_inc(b1["c_out"], 1)
                act.wait_ge(b1["c_in"], 2)
                act.activation(bt[0:8, 0, :], bt[0:8, 0, :], ACT.Ln).then_inc(b1["c_out"], 1)
                act.wait_ge(fox_c_ready, 1)
                act.dma_start(nc_row[0:1, :, :], cf[0:8, :]).then_inc(fox_c_landed, 16)
                attend("fox", block1, FOX_MAPS, 4)
                for d in range(4, 8):
                    fill_hi("out", d)

            for g in range(N_SPLIT):
                hi(g, D)
            act.wait_ge(c_landed, 16)
            act.activation(cond[:, :], cond[:, :], ACT.Silu).then_inc(cond_ready, 1)
            act.wait_ge(const_ready, 1)
            for stage in run:
                if stage == "in":
                    act.wait_ge(x_landed, 16)
                    for d in range(KT):
                        square(0, d, x[:, d, :])
                    std(0)
                    for d in range(KT):
                        fill_hi(stage, d)
                    m = 0
                    for j, kind in enumerate(IN_KINDS):
                        hi_ahead(stage, j)
                        if kind == "gelu_tok":
                            if m >= 2:
                                act.wait_ge(tok_T, m - 1)
                            evac_unit(stage, j, ACT.Gelu_apprx_tanh, sq[m % 2][:, :]).then_inc(bank_free[j % N_BANKS], 1)
                        elif kind in ("gelu", "silu"):
                            evac_unit(stage, j, ACT.Gelu_apprx_tanh if kind == "gelu" else ACT.Silu,
                                      in_dst(j)).then_inc(bank_free[j % N_BANKS], 1)
                        m += kind.endswith("tok")
                elif stage == "out":
                    block1_mixers()
                    for j in range(KT):
                        hi_ahead(stage, j)
                        act.wait_ge(*read_of(stage, j))
                        square(1, j, x[:, j, :])
                    std(1)
                elif stage.startswith("ffn"):
                    ffn(stage)
                elif stage in ("dsa", "diff"):
                    kinds = DSA_KINDS if stage == "dsa" else DIFF_KINDS
                    act.wait_ge(unit_done, UNIT_BASE[stage])
                    dst = {"dsa": dshuf[0], "diff": fshuf[0]}[stage]
                    act.dma_start(dst[:, :].bitcast(I32), A["pos"].partition_broadcast(P)).then_inc(
                        rope[stage]["pos_landed"], 16)
                    if stage == "diff":
                        act.dma_start(lam_in[:, :, :].rearrange("p a b -> p (a b)"),
                                      A["lam"].partition_broadcast(P)).then_inc(lam_landed, 16)
                    pre(stage)
                    r = rope[stage]
                    cs, sn, sh = (dcos, dsin, dshuf) if stage == "dsa" else (fcos, fsin, fshuf)
                    act.wait_ge(r["angle"], 1)
                    act.activation(sn[:, :], sn[:, :], ACT.Sin).then_inc(r["table"], 1)
                    act.wait_ge(r["angle"], 2)
                    act.activation(cs[:, :], cs[:, :], ACT.Sin).then_inc(r["table"], 1)
                    for j, kind in enumerate(kinds):
                        hi_ahead(stage, j)
                        if kind == "rope":
                            act.wait_ge(unit_done, UNIT_BASE[stage] + j + 1)
                            act.activation(rope_dst(stage, j), bank[j % N_BANKS][:, :], ACT.Copy).then_inc(bank_free[j % N_BANKS], 1)
                    if stage == "dsa":
                        for qb in range(1, NT):
                            for h in range(8):
                                n = 8 * (qb - 1) + h
                                act.wait_ge(ix["logit"], n + 1)
                                if n >= 2:
                                    act.wait_ge(ix["read"], n - 1)
                                w = (qb + 1) * P
                                act.activation(rel[n % 2][:, 0:w], bank[n % 4][:, 0:w], ACT.Relu).then_inc(ix["relu"], 1)
                        attend("dsa", dsa, DSA_MAPS, 8)
                    else:
                        act.wait_ge(lam_sum, 1)
                        act.activation(lam_col[:, 0:2], lam_col[:, 0:2], ACT.Exp).then_inc(lam_exp, 1)
                        attend("diff", diff, DIFF_MAPS, 4)
                        act.wait_ge(att["diff"]["otok_done"], 1)
                        act.activation(sq_o[:, :, :], diff["otok"][:, :, :], ACT.Square).then_inc(sub_sq, 1)
                        act.wait_ge(sub_sum, 1)
                        act.activation(st_o[:, :], st_o[:, :], ACT.Sqrt, bias=eps_col[:, 0:1],
                                       scale=1.0 / P).then_inc(sub_std, 1)
                else:
                    sub = stage[:-4]
                    for d in range(KT):
                        fill_hi(stage, d)
                    for j in range(KT):
                        hi_ahead(stage, j)
                        y_square(sub, stage, j, j)
                    std(POST[sub])

        @block.tensor
        def _(pe):
            def unit(stage, j, b, uses, k0=0, nk=KT, start=True, stop=True, it=0, rhs=(h_hi, h_lo), k_wait=None):
                g = UNIT_BASE[stage] + j
                pe.wait_ge(lo_ready, g + 1 + 4 * it)
                if start and (not isinstance(it, int) or uses + it > 0):
                    pe.wait_ge(bank_free[b], uses + it)
                hi_, lo_ = w_hi[g % N_SPLIT], w_lo[g % N_SPLIT]
                for k in range(nk):
                    if k_wait is not None:
                        pe.wait_ge(hl_ready, k_wait + k + 1)
                    w = slice(k * P, (k + 1) * P)
                    pe.matmul(bank[b][:, :], hi_[:, w], rhs[0][:, k0 + k, :], start=start and k == 0, stop=False)
                    pe.matmul(bank[b][:, :], hi_[:, w], rhs[1][:, k0 + k, :], start=False, stop=False)
                    mm = pe.matmul(bank[b][:, :], lo_[:, w], rhs[0][:, k0 + k, :], start=False,
                                   stop=stop and k == nk - 1)
                mm.then_inc(unit_done, 1)

            def total(n):
                pe.wait_ge(sums_done, 9 * (n + 1))
                if n:
                    pe.wait_ge(rstd_ready, n)
                pe.matmul(bank[6][:, :], ones[:, :], acc[:, :], start=True, stop=True).then_inc(ss_ready, 1)

            def four_transposes(m, src):
                for n in range(NT):
                    mm = pe.transpose(bank[4 + m % 2][:, n * P:(n + 1) * P], src(n), ident[:, :])
                mm.then_inc(tok_T, 1)

            def projections(stage, kinds):
                m = TOK[stage]
                pending = None

                def flush():
                    m, j = pending
                    pe.wait_ge(*read_of(stage, j))
                    done = m - TOK[stage]
                    if done >= 2:
                        pe.wait_ge(tok_done, TOK_DONE[stage] + done - 1)
                    four_transposes(m, lambda n: sq[m % 2][:, n * P:(n + 1) * P])

                for j, kind in enumerate(kinds):
                    unit(stage, j, j % N_BANKS, BANK_USES[stage, "all"][j % N_BANKS] + j // N_BANKS,
                         k_wait=8 * FILL[stage] if j == 0 else None)
                    if pending is not None:
                        flush()
                        pending = None
                    if kind.endswith("tok"):
                        pending = (m, j)
                        m += 1
                if pending is not None:
                    flush()

            def attend(k, cfg, maps, rounds):
                s = att[k]
                B = len(maps)
                vd = P if k == "diff" else HD
                with pe.Fori(0, rounds) as it:
                    pe.wait_ge(s["qs_ready"], it + 1)

                    def scores(u):
                        half, comp, qb = maps[u]
                        w = (qb + 1) * P
                        rows = slice(half * HD, half * HD + HD)
                        if u >= 4:
                            pe.wait_ge(s["p_ready"], B * it + u - 3)
                        if k == "dsa":
                            keys = cfg["k"][rows, 0:w]
                        else:
                            keys = cfg["ks"][rows, comp, 0:w]
                        out_ = bank[u % 4]
                        pe.matmul(out_[:, 0:w], cfg["qs"][rows, comp, qb * P:(qb + 1) * P], keys,
                                  start=True, stop=False)
                        if k == "fox":
                            pe.matmul(out_[:, 0:w], ones[0:1, :],
                                      nc_row[0:1, ds(2 * it + half, 1), 0:w].rearrange("p a n -> p (a n)"),
                                      start=False, stop=False)
                        if k == "dsa":
                            mm = pe.matmul(out_[:, 0:w], ident_bf[:, :], mask[:, qb, 0:w], start=False, stop=True)
                        else:
                            mm = pe.matmul(out_[:, qb * P:w], ident_bf[:, :], causal_bf[:, :], start=False, stop=True)
                        mm.then_inc(s["s_ready"], 1)

                    def transposes(u):
                        qb = maps[u][2]
                        pe.wait_ge(s["p_ready"], B * it + u + 1)
                        for sblk in range(qb + 1):
                            mm = pe.transpose(bank[4 + u % 2][:, sblk * P:(sblk + 1) * P],
                                              cfg["P"][:, u % 4, sblk * P:(sblk + 1) * P], ident[:, :])
                        mm.then_inc(s["tr_ready"], 1)

                    def values(u):
                        half, comp, qb = maps[u]
                        pe.wait_ge(s["pt_act" if u % 2 == 0 else "pt_dve"], (B // 2) * it + u // 2 + 1)
                        if u >= 2:
                            pe.wait_ge(s["o_read"], B * it + (u - u % 2 if k == "diff" else u - 1))
                        for sblk in range(qb + 1):
                            if k == "dsa":
                                v = cfg["v"][:, sblk, 0:HD]
                            elif k == "fox":
                                v = cfg["v"][:, sblk, ds(it * P + half * HD, HD)]
                            else:
                                v = cfg["v"][:, sblk, ds(it * 2 * P + half * P, P)]
                            mm = pe.matmul(bank[6 + u % 2][:, 0:vd], cfg["PT"][:, u % 2, sblk * P:(sblk + 1) * P], v,
                                           start=sblk == 0, stop=sblk == qb)
                        mm.then_inc(s["o_ready"], 1)

                    scores(0)
                    scores(1)
                    for u in range(B):
                        if u + 2 < B:
                            scores(u + 2)
                        transposes(u)
                        if u:
                            values(u - 1)
                    values(B - 1)

            def turn_back(stage, otok, count, d0=0):
                m0 = TOK[stage]
                for ft in range(count):
                    if ft >= 2:
                        pe.wait_ge(t_ready, 8 * FILL[stage if stage != "fox_out" else "out"] + d0 + ft - 1)
                    four_transposes(m0 + ft, lambda n: otok[:, n, ft * P:(ft + 1) * P])

            def block1_mixers():
                pe.wait_ge(b1["ws"], 1)
                pe.wait_ge(b1["vn"], 1)
                for g in range(4):
                    for n in range(NT):
                        mm = pe.matmul(bank[6 + g // 2][g % 2 * HD:g % 2 * HD + HD, n * P:(n + 1) * P],
                                       av[:, n, g * HD:(g + 1) * HD], ws[:, g, :], start=True, stop=True)
                mm.then_inc(b1["mixed"], 1)
                pe.wait_ge(b1["kh"], 1)
                for a in range(2):
                    for n in range(NT):
                        mm = pe.transpose(bank[4 + a][:, n * P:(n + 1) * P], bx[:, a, n * P:(n + 1) * P], ident[:, :])
                    mm.then_inc(b1["kh_T"], 1)
                pe.wait_ge(b1["kh_tok"], 2)
                for n in range(3):
                    for h in range(4):
                        r = slice(h % 2 * HD, h % 2 * HD + HD)
                        c = (n * 2 + h // 2) * HD
                        mm = pe.matmul(bank[6][r, c:c + HD], kh_tok[:, n, h * HD:(h + 1) * HD],
                                       bi[:, n, h * HD:(h + 1) * HD], start=True, stop=True)
                mm.then_inc(b1["kv"], 1)
                for i in range(8):
                    if i < 7:
                        pe.wait_ge(b1["x"], i + 1)
                        keys = queries = bf if i % 2 == 0 else bx
                    else:
                        keys, queries = bk, bq
                    for h in range(4):
                        r = slice(h % 2 * HD, h % 2 * HD + HD)
                        if i:
                            pe.wait_ge(b1["copied"], 4 * (i - 1) + h + 1)
                        for n in range(NT):
                            c = slice(n * P, (n + 1) * P)
                            mm = pe.matmul(bank[h][:, c], keys[r, h // 2, c], queries[r, h // 2, c],
                                           start=True, stop=True)
                        mm.then_inc(b1["levels"], 1)
                pe.wait_ge(b1["copied"], 32)
                pe.wait_ge(b1["state"], 1)
                for a in range(2):
                    for h in (2 * a, 2 * a + 1):
                        r = slice(h % 2 * HD, h % 2 * HD + HD)
                        for n in range(NT):
                            c = slice(n * P, (n + 1) * P)
                            mm = pe.matmul(bank[4 + a][r, c], bi[:, n, h * HD:(h + 1) * HD], sc[:, h, c],
                                           start=True, stop=n == 0)
                            if n:
                                mm = pe.matmul(bank[4 + a][r, c], state[r, n - 1, a, :], bt[r, a, c],
                                               start=False, stop=True)
                    mm.then_inc(b1["o"], 1)
                pe.wait_ge(b1["bd"], 1)
                for a in range(2):
                    pe.wait_ge(b1["osq"], a + 1)
                    pe.matmul(bank[6 + a][:, :], ws[:, 0, :], bx[:, a, :], start=True, stop=True).then_inc(b1["oss"], 1)
                pe.wait_ge(fox_c_landed, 16)
                pe.wait_ge(hl_ready, 8 * FILL["out"] + 4)
                attend("fox", block1, FOX_MAPS, 4)
                pe.wait_ge(att["fox"]["otok_done"], 1)
                turn_back("fox_out", block1["otok"], 4, d0=4)

            pe.wait_ge(const_ready, 1)
            for stage in run:
                if stage == "in":
                    total(0)
                    projections(stage, IN_KINDS)
                elif stage == "out":
                    block1_mixers()
                    for j in range(KT):
                        unit(stage, j, j % N_BANKS, BANK_USES[stage, "all"][j % N_BANKS] + j // N_BANKS,
                             k_wait=8 * FILL[stage] if j == 0 else None)
                    total(1)
                elif stage.startswith("ffn"):
                    total(PRE[stage])
                    pe.wait_ge(hl_ready, 8 * FILL[stage] + 8)
                    with pe.Fori(0, 2 * FT // 4) as it:
                        for j in range(4):
                            unit(stage, j, j, BANK_USES[stage, "up"][j], it=it)
                    pe.wait_ge(alo_ready, FT * (ffn_no(stage) + 1))
                    with pe.Fori(0, 2 * KT // 4) as it:
                        for j in range(4):
                            unit(stage, 2 * FT + j, j // 2, BANK_USES[stage, "down"][j // 2], k0=FH * (j % 2), nk=FH,
                                 start=j % 2 == 0, stop=j % 2 == 1, it=it, rhs=(a_hi, a_lo))
                    total(POST[stage])
                elif stage in ("dsa", "diff"):
                    total(PRE[stage])
                    projections(stage, DSA_KINDS if stage == "dsa" else DIFF_KINDS)
                    pe.wait_ge(rope[stage]["done"], 1)
                    if stage == "dsa":
                        for qb in range(1, NT):
                            for h in range(8):
                                n = 8 * (qb - 1) + h
                                r = slice(h % 2 * HD, h % 2 * HD + HD)
                                w = (qb + 1) * P
                                if n >= 4:
                                    pe.wait_ge(ix["relu"], n - 3)
                                pe.matmul(bank[n % 4][:, 0:w], dqi[r, h // 2, qb * P:(qb + 1) * P], dki[r, 0:w],
                                          start=True, stop=True).then_inc(ix["logit"], 1)
                        pe.wait_ge(ix["mask"], 1)
                        attend("dsa", dsa, DSA_MAPS, 8)
                    else:
                        attend("diff", diff, DIFF_MAPS, 4)
                else:
                    sub = stage[:-4]
                    otok = (dsa if sub == "dsa" else diff)["otok"]
                    pe.wait_ge(att[sub]["otok_done"], 1 if sub == "dsa" else 2)
                    turn_back(stage, otok, KT)
                    for j in range(KT):
                        unit(stage, j, j % N_BANKS, BANK_USES[stage, "all"][j % N_BANKS] + j // N_BANKS,
                             k_wait=8 * FILL[stage] if j == 0 else None)
                    total(POST[sub])

        @block.gpsimd
        def _(pool):
            def add_square(n, d, it_d=0):
                pool.wait_ge(sq_ready, 8 * n + d + 1 + it_d)
                pool.wait_ge(sums_done, 9 * n + d + 1 + it_d)
                pool.tensor_tensor(acc[:, :], acc[:, :], sq[d % 2][:, :], ALU.add).then_inc(sums_done, 1)

            def clear(n):
                if n:
                    pool.wait_ge(ss_ready, n)
                pool.memset(acc[:, :], 0.0).then_inc(sums_done, 1)

            def sums(n):
                clear(n)
                for d in range(KT):
                    add_square(n, d)

            def residual(i, after=None):
                for d in range(KT):
                    pool.wait_ge(u_ready, 8 * i + d + 1)
                    pool.tensor_tensor(x[:, d, :], x[:, d, :], t[d % 2][:, :], ALU.add).then_inc(x_pool, 1)

            def load_ada(n, parity):
                if not (isinstance(n, int) and n < 2):
                    pool.wait_ge(ada_used, n - 1)
                pool.dma_start(ada[parity][:, :], A["ada"][ds(n, 1)].rearrange("a p n -> (a p) n")).then_inc(
                    ada_landed[parity], 16)

            def load_static(stage):
                for j in range(dict(STAGE_UNITS)[stage]):
                    for n in ada_of(stage, j):
                        load_ada(n, n % 2)

            for stage in run:
                if stage == "in":
                    sums(0)
                    pool.wait_ge(b1_landed, 16 * 9)
                    pool.affine_select(out=ws[:, :, :], in_=ws[:, :, :], compare_op=ALU.is_ge, fill=0.0, base=0,
                                       pattern=[[0, 4], [1, P]], channel_multiplier=-1).then_inc(b1["ws"], 1)
                    load_static(stage)
                elif stage == "out":
                    clear(1)
                    for j in range(KT):
                        for n in ada_of(stage, j):
                            load_ada(n, n % 2)
                        add_square(1, j)
                elif stage.startswith("ffn"):
                    i = SUBS.index(stage)
                    sums(PRE[stage])
                    for first, count, with_ada, part in loops(stage):
                        if part == "up" and with_ada:
                            with pool.Fori(0, count) as it:
                                for j in range(4):
                                    load_ada(ada_index(stage, first, j, it), (first + j) % 2)
                        elif part == "down":
                            clear(POST[stage])
                            with pool.Fori(0, count) as it:
                                for d in range(2):
                                    for j in (2 * d, 2 * d + 1):
                                        if with_ada:
                                            load_ada(ada_index(stage, first, j, it), (first + j) % 2)
                                    add_square(POST[stage], d, 2 * it)
                    residual(i)
                elif stage in ("dsa", "diff"):
                    sums(PRE[stage])
                else:
                    sums(POST[stage[:-4]])
                    residual(SUBS.index(stage[:-4]))

        @block.vector
        def _(dve):
            chain = Chain(dve, dve_step)
            link = chain.link

            def lo(g, w, it=0):
                dve.wait_ge(hi_ready, g + 1 + 4 * it)
                dve.tensor_tensor(w_lo[g % N_SPLIT][:, 0:w], raw[g % N_RAW][:, 0:w],
                                  w_hi[g % N_SPLIT][:, 0:w].bitcast(F32), ALU.subtract).then_inc(lo_ready, 1)

            def lo_ahead(stage, j, it=0):
                g = UNIT_BASE[stage] + j + N_SPLIT
                if not isinstance(it, int):
                    lo(g, raw_width(stage, j), it)
                elif g + 4 * it < n_units:
                    lo(g, width_of(g + 4 * it), it)

            def mod_tile(n, parity, landed):
                dve.wait_ge(ada_landed[parity], landed)
                dve.scalar_tensor_tensor(out=ada[parity][:, :], in0=ada[parity][:, :], scalar=1.0, in1=cond[:, :],
                                         op0=ALU.mult, op1=ALU.mult,
                                         accum_out=mod_raw[:, ds(n, 1)]).then_inc(ada_used, 1)

            def mod_static(stage, j):
                for n in ada_of(stage, j):
                    mod_tile(n, n % 2, 16 * (n // 2 + 1))

            def mod_loop(stage, j, it):
                n = MOD_TILES + j + (0 if stage == "ffn0" else 2 * FT + 2 * KT)
                mod_tile(n + 4 * it, n % 2, 16 * (n // 2 + 1) + 32 * it)

            def finish_modulation(layer):
                dve.wait_ge(ada_used, MOD_TILES * (layer + 1))
                c0 = layer * MOD_TILES
                link(dve.tensor_tensor(mod_raw[:, c0:c0 + MOD_TILES], mod_raw[:, c0:c0 + MOD_TILES],
                                       cols[:, COL["ada_b"] + c0:COL["ada_b"] + c0 + MOD_TILES], ALU.add))
                for i in range(3 * layer, 3 * layer + 3):
                    at = c0 + 3 * (i % 3) * KT
                    c = slice(i * KT, (i + 1) * KT)
                    dve.scalar_tensor_tensor(out=gain[:, c], in0=mod_raw[:, at + KT:at + 2 * KT], scalar=1.0,
                                             in1=cols[:, COL["pre"] + i * KT:COL["pre"] + (i + 1) * KT],
                                             op0=ALU.add, op1=ALU.mult)
                    link(dve.scalar_tensor_tensor(out=coef[:, c], in0=mod_raw[:, at + 2 * KT:at + 3 * KT],
                                                  scalar=1.0 if i % 3 == 1 else 0.5,
                                                  in1=cols[:, COL["post"] + i * KT:COL["post"] + (i + 1) * KT],
                                                  op0=ALU.mult, op1=ALU.mult))

            def inverse(n):
                dve.wait_ge(sqrt_done, n + 1)
                dve.reciprocal(rstd[:, :], rstd[:, :]).then_inc(rstd_ready, 1)
                dve.wait_ge(rstd_ready, n + 1)

            def fill(stage, produce, tiles=range(KT), bias=None):
                tiles = list(tiles)
                for i in range(len(tiles) + 1):
                    if i < len(tiles):
                        if i >= 2:
                            dve.wait_ge(hl_ready, 8 * FILL[stage] + tiles[i - 2] + 1)
                        produce(tiles[i], t[tiles[i] % 2]).then_inc(t_ready, 1)
                    if i:
                        d = tiles[i - 1]
                        dve.wait_ge(hh_ready, 8 * FILL[stage] + d + 1)
                        dve.scalar_tensor_tensor(out=h_lo[:, d, :], in0=t[d % 2][:, :],
                                                 scalar=0.0 if bias is None else bias(d),
                                                 in1=h_hi[:, d, :].bitcast(F32), op0=ALU.add,
                                                 op1=ALU.subtract).then_inc(hl_ready, 1)

            def normed(gains, at):
                return lambda d, out_: dve.scalar_tensor_tensor(
                    out=out_[:, :], in0=x[:, d, :], scalar=gains[:, at + d:at + d + 1], in1=rstd[:, :],
                    op0=ALU.mult, op1=ALU.mult)

            def pre(stage):
                i = SUBS.index(stage)
                inverse(PRE[stage])
                fill(stage, normed(gain, i * KT), bias=lambda d: shift_col(i, d))

            def post(stage):
                i = SUBS.index(stage)
                inverse(POST[stage])
                for d in range(KT):
                    if 8 * i + d >= 2:
                        dve.wait_ge(x_pool, 8 * i + (d - 1 if d >= 2 else 0))
                    dve.scalar_tensor_tensor(out=t[d % 2][:, :], in0=y_of(stage)[:, d, :], scalar=coef[:, i * KT + d:i * KT + d + 1],
                                             in1=rstd[:, :], op0=ALU.mult, op1=ALU.mult).then_inc(u_ready, 1)

            def ffn(stage):
                pre(stage)
                for first, count, with_ada, part in loops(stage):
                    def up(it):
                        for f in range(2):
                            j = first + 2 * f
                            lo_ahead(stage, j, it)
                            if with_ada:
                                mod_loop(stage, j, it)
                            lo_ahead(stage, j + 1, it)
                            if with_ada:
                                mod_loop(stage, j + 1, it)
                            fi = first // 2 + f + 2 * it
                            dve.wait_ge(*read_of(stage, j, it))
                            dve.wait_ge(unit_done, UNIT_BASE[stage] + j + 2 + 4 * it)
                            dve.tensor_tensor(t[f][:, :], sq[f][:, :], bank[2 * f + 1][:, :],
                                              ALU.mult).then_inc(bank_free[2 * f + 1], 1)
                            dve.wait_ge(ahi_ready, FT * ffn_no(stage) + fi + 1)
                            dve.tensor_tensor(a_lo[:, ds(fi, 1), :].rearrange("p a n -> p (a n)"), t[f][:, :],
                                              a_hi[:, ds(fi, 1), :].rearrange("p a n -> p (a n)").bitcast(F32),
                                              ALU.subtract).then_inc(alo_ready, 1)

                    def down(it):
                        for d in range(2):
                            j = first + 2 * d
                            lo_ahead(stage, j, it)
                            if with_ada:
                                mod_loop(stage, j, it)
                            lo_ahead(stage, j + 1, it)
                            if with_ada:
                                mod_loop(stage, j + 1, it)
                            dve.wait_ge(unit_done, UNIT_BASE[stage] + j + 2 + 4 * it)
                            dve.tensor_copy(y[:, ds(2 * it + d, 1), :].rearrange("p a n -> p (a n)"),
                                            bank[d][:, :]).then_inc(bank_free[d], 1)
                    bodies(dve, count, up if part == "up" else down)
                post(stage)

            def projections(stage, kinds, on_tile):
                m, pending = TOK[stage], None

                def flush():
                    m_, j_ = pending
                    dve.wait_ge(tok_T, m_ + 1)
                    dve.tensor_copy(tok_dst(stage, j_), bank[4 + m_ % 2][:, :].rearrange("p (n c) -> p n c", n=NT)
                                    ).then_inc(tok_done, 1)
                for j, kind in enumerate(kinds):
                    lo_ahead(stage, j)
                    mod_static(stage, j)
                    if kind in ("copy", "tok"):
                        dve.wait_ge(unit_done, UNIT_BASE[stage] + j + 1)
                        if kind == "tok" and m - TOK[stage] >= 2:
                            dve.wait_ge(tok_T, m - 1)
                        dve.tensor_copy(sq[m % 2][:, :] if kind == "tok" else in_dst(j),
                                        bank[j % N_BANKS][:, :]).then_inc(bank_free[j % N_BANKS], 1)
                    elif kind == "rope":
                        on_tile(j)
                    if pending is not None:
                        flush()
                        pending = None
                    if kind.endswith("tok"):
                        pending = (m, j)
                        m += 1
                if pending is not None:
                    flush()
                dve.wait_ge(tok_done, TOK_DONE[stage] + m - TOK[stage])

            def rope_tables(stage):
                r = rope[stage]
                cs, sn, sh = (dcos, dsin, dshuf) if stage == "dsa" else (fcos, fsin, fshuf)
                turn = 2 * np.pi
                c1 = 6.28125
                c2 = float(np.float32(int((turn - c1) * 2 ** 22) / 2 ** 22))
                c3 = float(turn - c1 - c2)
                magic = 1.5 * 2.0 ** 23
                dve.wait_ge(r["pos_landed"], 16)
                link(dve.tensor_copy(sh[1][:, :], sh[0][:, :].bitcast(I32)))
                link(dve.tensor_scalar(sh[1][:, :], sh[1][:, :], cols[:, COL["inv_freq"]:COL["inv_freq"] + 1], None, ALU.mult))
                link(dve.tensor_scalar(sh[0][:, :], sh[1][:, :], 1.0 / turn, magic, ALU.mult, ALU.add))
                link(dve.tensor_scalar(sh[0][:, :], sh[0][:, :], -magic, None, ALU.add))
                for c in (c1, c2, c3):
                    link(dve.scalar_tensor_tensor(out=sh[1][:, :], in0=sh[0][:, :], scalar=-c, in1=sh[1][:, :],
                                                  op0=ALU.mult, op1=ALU.add))
                below = float(np.nextafter(np.float32(np.pi), np.float32(0)))
                dve.tensor_scalar(sn[:, :], sh[1][:, :], below, -below, ALU.min, ALU.max).then_inc(r["angle"], 1)
                dve.wait_ge(r["angle"], 1)
                link(dve.scalar_tensor_tensor(out=cs[:, :], in0=sh[1][:, :], scalar=-1.0, in1=sh[1][:, :],
                                              op0=ALU.mult, op1=ALU.min))
                dve.tensor_scalar(cs[:, :], cs[:, :], float(np.pi / 2), None, ALU.add).then_inc(r["angle"], 1)
                dve.wait_ge(r["table"], 1)
                link(dve.tensor_scalar(sn[:, :], sn[:, :], cols[:, COL["sign"]:COL["sign"] + 1], None, ALU.mult))
                dve.wait_ge(r["table"], 2)

            def rotate(stage, j):
                cs, sn, sh = (dcos, dsin, dshuf) if stage == "dsa" else (fcos, fsin, fshuf)
                q = rope_dst(stage, j)
                s_ = sh[j % 2][:, :]
                dve.wait_ge(*read_of(stage, j))
                swap = [(i + 8) % 16 if i < 16 else i for i in range(32)]
                link(dve.stream_shuffle(s_, q, swap))
                link(dve.tensor_tensor(s_, s_, sn[:, :], ALU.mult))
                link(dve.tensor_tensor(q, q, cs[:, :], ALU.mult))
                link(dve.tensor_tensor(q, q, s_, ALU.add))

            def attend(k, cfg, maps, rounds):
                s = att[k]
                B = len(maps)
                s_t = cfg["st"]
                comps = 2 if k == "diff" else 1
                with dve.Fori(0, rounds) as it:
                    chain.body(it, B)
                    for c in range(comps):
                        if k != "dsa":
                            dve.tensor_copy(cfg["ks"][:, c, :],
                                            cfg["k"][:, ds(it + 4 * c, 1), :].rearrange("p a n -> p (a n)"))
                        ins = dve.tensor_scalar(cfg["qs"][:, c, :],
                                                cfg["q"][:, ds(it + 4 * c, 1), :].rearrange("p a n -> p (a n)"),
                                                HD ** -0.5, None, ALU.mult)
                    ins.then_inc(s["qs_ready"], 1)

                    def row_max(u):
                        w = (maps[u][2] + 1) * P
                        dve.wait_ge(s["s_ready"], B * it + u + 1)
                        dve.tensor_reduce(s_t[:, 0, u:u + 1], bank[u % 4][:, 0:w], AX, ALU.max,
                                          negate=True).then_inc(s["nm_ready"], 1)

                    def output(u):
                        half, comp, qb = maps[u]
                        if k != "diff":
                            dve.wait_ge(s["o_ready"], B * it + u + 1)
                            link(dve.reciprocal(s_t[:, 2, u:u + 1], s_t[:, 1, u:u + 1]))
                            dve.tensor_scalar(cfg["otok"][:, qb, ds(it * P + half * HD, HD)], bank[6 + u % 2][:, 0:HD],
                                              s_t[:, 2, u:u + 1], None, ALU.mult).then_inc(s["o_read"], 1)
                        elif comp == 1:
                            dve.wait_ge(s["o_ready"], B * it + u + 1)
                            link(dve.reciprocal(s_t[:, 2, u - 1:u + 1], s_t[:, 1, u - 1:u + 1]))
                            link(dve.tensor_scalar(s_t[:, 2, u:u + 1], s_t[:, 2, u:u + 1], lam_col[:, 2:3], None, ALU.mult))
                            o_t = cfg["ot"]
                            dve.tensor_scalar(o_t[:, :], bank[7][:, 0:P], s_t[:, 2, u:u + 1], None,
                                              ALU.mult).then_inc(s["o_read"], 1)
                            dve.wait_ge(s["o_read"], B * it + u)
                            dve.scalar_tensor_tensor(out=cfg["otok"][:, qb, ds(it * 2 * P + half * P, P)],
                                                     in0=bank[6][:, 0:P], scalar=s_t[:, 2, u - 1:u], in1=o_t[:, :],
                                                     op0=ALU.mult, op1=ALU.subtract).then_inc(s["o_read"], 1)
                    row_max(0)
                    row_max(1)
                    for u in range(B):
                        if u + 2 < B:
                            row_max(u + 2)
                        if u % 2:
                            w = (maps[u][2] + 1) * P
                            dve.wait_ge(s["tr_ready"], B * it + u + 1)
                            if u >= 2:
                                dve.wait_ge(s["o_ready"], B * it + u - 1)
                            dve.tensor_copy(cfg["PT"][:, 1, 0:w], bank[5][:, 0:w]).then_inc(s["pt_dve"], 1)
                        if u:
                            output(u - 1)
                    output(B - 1)
                chain.leave(rounds)
                dve.wait_ge(s["o_read"], B * rounds)
                dve.tensor_copy(s_t[:, 2, 0:1], s_t[:, 1, 0:1]).then_inc(s["otok_done"], 1)

            def block1_mixers():
                dve.wait_ge(b1_landed, 16 * 9)
                link(dve.tensor_copy(level[:, :, :], level_raw[:, :, :]))
                groups = av[:, :, :].rearrange("p n (g c) -> p (n g) c", c=HD)

                def over(c):
                    return st[:, c, :].unsqueeze(2).broadcast_to([P, 16, HD])
                link(dve.tensor_reduce(st[:, 0, :], groups, AX, ALU.add))
                link(dve.tensor_scalar(st[:, 1, :], st[:, 0, :], 1.0 / HD, None, ALU.mult))
                link(dve.tensor_tensor(groups, groups, over(1), ALU.subtract))
                bxg = bx[:, :, :].rearrange("p a (b c) -> p (a b) c", c=HD)
                link(dve.tensor_tensor(bxg, groups, groups, ALU.mult))
                dve.tensor_reduce(st[:, 2, :], bxg, AX, ALU.add).then_inc(b1["var"], 1)
                dve.wait_ge(b1["std"], 1)
                link(dve.reciprocal(st[:, 3, :], st[:, 3, :]))
                link(dve.tensor_tensor(groups, groups, over(3), ALU.mult))
                rows = [P, NT, 256]
                link(dve.tensor_tensor(av[:, :, :], av[:, :, :], ln_g[:, :].unsqueeze(1).broadcast_to(rows), ALU.mult))
                dve.tensor_tensor(av[:, :, :], av[:, :, :], ln_b[:, :].unsqueeze(1).broadcast_to(rows),
                                  ALU.add).then_inc(b1["vn"], 1)
                lb = cols[:, COL["lb"]:COL["lb"] + 2]
                dve.tensor_tensor(bcol[:, 0:2], lb, lb, ALU.subtract).then_inc(b1["lb"], 1)
                dve.wait_ge(b1["mixed"], 1)

                def mixed(d, out_):
                    b = bank[6 + d][:, :].rearrange("p (n s) -> p n s", n=NT)
                    u = bx[:, d, :]
                    link(dve.tensor_tensor(u.rearrange("p (n s) -> p n s", n=NT), b,
                                           bs_bc[:, d, :].unsqueeze(1).broadcast_to([P, NT, P]), ALU.add))
                    link(dve.tensor_tensor(u, u, au[:, d, :], ALU.mult))
                    return dve.tensor_tensor(out_[:, :], u, az[:, d, :], ALU.mult)
                fill("out", mixed, range(0, 2))

                dve.wait_ge(b1["lb_exp"], 1)
                link(dve.reciprocal(bcol[:, 4:6], bcol[:, 2:4]))
                link(dve.tensor_tensor(bcol[:, 2:4], bcol[:, 2:4], bcol[:, 4:6], ALU.mult))
                link(dve.tensor_tensor(bcol[:, 4:6], bcol[:, 2:4], bcol[:, 2:4], ALU.subtract))
                link(dve.tensor_scalar(bcol[:, 4:6], bcol[:, 4:6], 0.0, 1.0 - 1e-6, ALU.max, ALU.min))
                link(dve.tensor_scalar(bcol[:, 6:8], bcol[:, 4:6], -1.0, 1.0, ALU.mult, ALU.add))
                dve.wait_ge(b1["exps"], 2)
                link(dve.tensor_scalar(bk[:, :, :], bk[:, :, :], 1.0, None, ALU.add))
                link(dve.reciprocal(bk[:, :, :], bk[:, :, :]))
                link(dve.tensor_scalar(bt[:, :, :], bt[:, :, :], 1.0, None, ALU.add))
                link(dve.reciprocal(bt[:, :, :], bt[:, :, :]))
                for a in range(2):
                    dve.tensor_scalar(bk[:, a, :], bk[:, a, :], bcol[:, 6 + a:7 + a], None, ALU.mult)
                    link(dve.tensor_scalar(bt[:, a, :], bt[:, a, :], bcol[:, 6 + a:7 + a], bcol[:, 4 + a:5 + a],
                                           ALU.mult, ALU.add))
                link(dve.tensor_scalar(bt[:, :, :], bt[:, :, :], F_FLOOR, None, ALU.max))
                link(dve.tensor_scalar(bx[:, :, :], bt[:, :, :], 2.0 ** -40, 2.0 ** 60, ALU.is_lt, ALU.mult))
                link(dve.tensor_scalar(bx[:, :, :], bx[:, :, :], 1.0, None, ALU.max))
                dve.tensor_tensor(bf[:, :, :], bx[:, :, :], bt[:, :, :], ALU.mult).then_inc(b1["f"], 1)
                dve.wait_ge(b1["f"], 1)
                link(dve.tensor_scalar(bx[:, :, :], bt[:, :, :], 2.0 ** -40, float(-60 * np.log(2.0)), ALU.is_lt, ALU.mult))
                dve.wait_ge(b1["ln"], 1)
                link(dve.tensor_tensor(bx[:, :, :], bx[:, :, :], bf[:, :, :], ALU.add))
                for a in range(2):
                    ins = dve.tensor_tensor_scan(bb[:, a, :], keep, bx[:, a, :], 0.0, ALU.mult, ALU.add)
                    if a == 0:
                        link(ins)
                ins.then_inc(b1["b"], 1)
                link(dve.tensor_scalar(bq[:, :, :], bq[:, :, :], HD ** -0.5, None, ALU.mult))
                dve.wait_ge(b1["b"], 1)
                chunks = bb[:, :, :].rearrange("p a (n s) -> p (a n) s", s=P)
                xc = bx[:, :, :].rearrange("p a (n s) -> p (a n) s", s=P)
                link_x = xc
                dve.tensor_tensor(link_x, chunks[:, :, P - 1:P].broadcast_to([P, 8, P]), chunks,
                                  ALU.subtract).then_inc(b1["e_in"], 1)
                dve.memset(sc[:, :, :], 0.0).then_inc(b1["sc"], 1)
                dve.wait_ge(b1["e_out"], 2)
                link(dve.tensor_tensor(bt[:, :, :], bt[:, :, :], bq[:, :, :], ALU.mult))
                dve.wait_ge(b1["e_out"], 3)
                dve.tensor_tensor(bx[:, :, :], bx[:, :, :], bk[:, :, :], ALU.mult).then_inc(b1["kh"], 1)

                def level_views(buf, m):
                    v = buf[:, :, :].rearrange("p a (n s) -> p (a n) s", s=2 * m)
                    return v[:, :, 0:m], v[:, :, m:2 * m], v[:, :, m - 1:m]

                def level_in(i):
                    m = P >> (i + 1)
                    dst = bf if i % 2 == 0 else bx
                    low, high, _ = level_views(dst, m)
                    b_low, b_high, mid = level_views(bb, m)
                    mid = mid.broadcast_to([P, D // (2 * m), m])
                    dve.tensor_tensor(low, mid, b_low, ALU.subtract)
                    dve.tensor_tensor(high, b_high, mid, ALU.subtract).then_inc(b1["e_in"], 1)

                def level_out(i):
                    m = P >> (i + 1)
                    dst = bf if i % 2 == 0 else bx
                    low, high, _ = level_views(dst, m)
                    k_low, _, _ = level_views(bk, m)
                    _, q_high, _ = level_views(bq, m)
                    dve.wait_ge(b1["e_out"], 4 + i)
                    dve.tensor_tensor(low, low, k_low, ALU.mult)
                    dve.tensor_tensor(high, high, q_high, ALU.mult).then_inc(b1["x"], 1)

                def take(i):
                    for h in range(4):
                        dve.wait_ge(b1["levels"], 4 * i + h + 1)
                        dve.copy_predicated(sc[:, h, :].rearrange("p (n s) -> p n s", n=NT),
                                            level[:, i, :].unsqueeze(1).broadcast_to([P, NT, P]),
                                            bank[h][:, :].rearrange("p (n s) -> p n s", n=NT)).then_inc(b1["copied"], 1)
                level_in(0)
                for a in range(2):
                    dve.wait_ge(b1["kh_T"], a + 1)
                    dve.tensor_copy(kh_tok[:, :, a * P:(a + 1) * P],
                                    bank[4 + a][:, :].rearrange("p (n s) -> p n s", n=NT)).then_inc(b1["kh_tok"], 1)
                level_out(0)
                level_in(1)
                dve.wait_ge(b1["kv"], 1)
                kv = bank[6][:, 0:3 * 2 * HD].rearrange("p (n a c) -> p n a c", n=3, a=2)
                link(dve.tensor_copy(state[:, 0, :, :], kv[:, 0, :, :]))
                for n in (1, 2):
                    for a in range(2):
                        ins = dve.scalar_tensor_tensor(out=state[:, n, a, :], in0=state[:, n - 1, a, :],
                                                       scalar=bcol[:, 8 + 4 * a + n:9 + 4 * a + n], in1=kv[:, n, a, :],
                                                       op0=ALU.mult, op1=ALU.add)
                        if (n, a) != (2, 1):
                            link(ins)
                ins.then_inc(b1["state"], 1)
                dve.wait_ge(b1["sc"], 1)
                for i in range(7):
                    if i:
                        level_out(i)
                    take(i)
                    if i + 2 < 7:
                        level_in(i + 2)
                take(7)
                link(dve.memset(ws[:, 0, :], 0.0))
                dve.memset(ws[0:HD, 0, 0:HD], 1.0)
                link(dve.memset(ws[HD:P, 0, HD:P], 1.0))
                dve.tensor_copy(bcol[:, 63:64], bcol[:, 8:9]).then_inc(b1["bd"], 1)
                dve.wait_ge(b1["ostd"], 2)
                link(dve.reciprocal(bt[:, :, :], bt[:, :, :]))

                def hgrn_out(d, out_):
                    a = d - 2
                    link(dve.scalar_tensor_tensor(out=bx[:, a, :], in0=bank[4 + a][:, :],
                                                  scalar=cols[:, COL["onorm"]:COL["onorm"] + 1], in1=bt[:, a, :],
                                                  op0=ALU.mult, op1=ALU.mult))
                    return dve.tensor_tensor(out_[:, :], bx[:, a, :], bz[:, a, :], ALU.mult)
                fill("out", hgrn_out, range(2, 4))

                s8, e8 = cf[0:8, :], bt[0:8, 0, :]
                link(dve.tensor_scalar(s8, s8, cols[0:8, COL["fox_b"]:COL["fox_b"] + 1], None, ALU.add))
                dve.scalar_tensor_tensor(out=e8, in0=s8, scalar=-1.0, in1=s8, op0=ALU.mult,
                                         op1=ALU.min).then_inc(b1["c_in"], 1)
                dve.wait_ge(b1["c_in"], 1)
                link(dve.tensor_scalar(s8, s8, 0.0, None, ALU.min))
                dve.wait_ge(b1["c_out"], 1)
                dve.tensor_scalar(e8, e8, 1.0, None, ALU.add).then_inc(b1["c_in"], 1)
                dve.memset(bt[0:8, 1, :], 1.0)
                dve.wait_ge(b1["c_out"], 2)
                link(dve.tensor_tensor(e8, e8, s8, ALU.subtract))
                dve.tensor_tensor_scan(s8, bt[0:8, 1, :], e8, 0.0, ALU.mult, ALU.add).then_inc(fox_c_ready, 1)
                attend("fox", block1, FOX_MAPS, 4)

                def fox_out(d, out_):
                    m = TOK["fox_out"] + d - 4
                    dve.wait_ge(tok_T, m + 1)
                    return dve.tensor_tensor(out_[:, :], bank[4 + m % 2][:, :], cz[:, d - 4, :], ALU.mult)
                fill("out", fox_out, range(4, 8))

            def select():
                link(dve.tensor_scalar(wi[:, :, :], dv[:, :, HD:HD + 8], float(8 ** -0.5 * HD ** -0.5), None, ALU.mult))
                link(dve.tensor_copy(mask[:, 0, 0:P], causal_bf[:, :]))
                for qb in range(1, NT):
                    w = (qb + 1) * P
                    s_ = [b[:, 0:w] for b in score]
                    for h in range(8):
                        n = 8 * (qb - 1) + h
                        dve.wait_ge(ix["relu"], n + 1)
                        r_ = rel[n % 2][:, 0:w]
                        if h == 0:
                            ins = dve.tensor_scalar(s_[0], r_, wi[:, qb, 0:1], None, ALU.mult)
                        else:
                            ins = dve.scalar_tensor_tensor(out=s_[0], in0=r_, scalar=wi[:, qb, h:h + 1], in1=s_[0],
                                                           op0=ALU.mult, op1=ALU.add)
                        ins.then_inc(ix["read"], 1)
                        dve.wait_ge(ix["read"], n + 1)
                    link(dve.tensor_tensor(score[0][:, qb * P:w], score[0][:, qb * P:w], causal_bf[:, :], ALU.add))
                    for r in range(TOPK // 8):
                        link(dve.max(top8[:, 0, :], s_[r % 2]))
                        link(dve.match_replace(s_[(r + 1) % 2], top8[:, 0, :], s_[r % 2], TAKEN))
                    ins = dve.tensor_scalar(mask[:, qb, 0:w], s_[0], TAKEN / 1.5, NEG, ALU.is_ge, ALU.mult)
                    if qb < NT - 1:
                        link(ins)
                ins.then_inc(ix["mask"], 1)

            def turned(stage, scale=None):
                def produce(d, out_):
                    m = TOK[stage] + d
                    dve.wait_ge(tok_T, m + 1)
                    if scale is None:
                        return dve.tensor_copy(out_[:, :], bank[4 + m % 2][:, :])
                    return dve.tensor_scalar(out_[:, :], bank[4 + m % 2][:, :], scale, 1.0 - LAM_INIT,
                                             ALU.mult, ALU.mult)
                return produce

            dve.memset(ones[:, :], 1.0)
            dve.memset(eps_col[:, :], EPS)
            dve.wait_ge(const_landed, 48)
            dve.tensor_copy(ident_bf[:, :], ident[:, :])
            dve.tensor_copy(causal_bf[:, :], t[0][:, 0:P]).then_inc(const_ready, 1)
            dve.wait_ge(const_ready, 1)
            for g in range(N_SPLIT):
                lo(g, D)
            dve.wait_ge(cond_ready, 1)
            for stage in run:
                if stage == "in":
                    inverse(0)
                    fill(stage, normed(cols, COL["norm_g"]))
                    projections(stage, IN_KINDS, None)
                elif stage == "out":
                    block1_mixers()
                    for j in range(KT):
                        lo_ahead(stage, j)
                        mod_static(stage, j)
                        dve.wait_ge(unit_done, UNIT_BASE[stage] + j + 1)
                        dve.tensor_tensor(x[:, j, :], x[:, j, :], bank[j % N_BANKS][:, :],
                                          ALU.add).then_inc(bank_free[j % N_BANKS], 1)
                    finish_modulation(0)
                    inverse(1)
                    for j in range(KT - N_BANKS, KT):
                        dve.wait_ge(*read_of(stage, j))
                    for d in range(KT):
                        normed(cols, COL["final_g"])(d, x[:, d, :]).then_inc(x_dve, 1)
                elif stage.startswith("ffn"):
                    if stage == "ffn2":
                        finish_modulation(1)
                    ffn(stage)
                elif stage in ("dsa", "diff"):
                    pre(stage)
                    rope_tables(stage)
                    projections(stage, DSA_KINDS if stage == "dsa" else DIFF_KINDS, lambda j: rotate(stage, j))
                    dve.memset(lam_col[:, 3:4], 0.0).then_inc(rope[stage]["done"], 1)
                    if stage == "dsa":
                        select()
                        attend("dsa", dsa, DSA_MAPS, 8)
                    else:
                        dve.wait_ge(lam_landed, 16)
                        for c in range(2):
                            link(dve.tensor_tensor(lam_in[:, 2 * c, :], lam_in[:, 2 * c, :], lam_in[:, 2 * c + 1, :], ALU.mult))
                            ins = dve.tensor_reduce(lam_col[:, c:c + 1], lam_in[:, 2 * c, :], AX, ALU.add)
                        ins.then_inc(lam_sum, 1)
                        dve.wait_ge(lam_exp, 1)
                        link(dve.scalar_tensor_tensor(out=lam_col[:, 2:3], in0=lam_col[:, 0:1], scalar=LAM_INIT,
                                                      in1=lam_col[:, 1:2], op0=ALU.add, op1=ALU.subtract))
                        attend("diff", diff, DIFF_MAPS, 4)
                        heads = diff["otok"][:, :, :].rearrange("p n (h c) -> p (n h) c", c=P)
                        dve.wait_ge(sub_sq, 1)
                        dve.tensor_reduce(st_o[:, :], sq_o[:, :, :].rearrange("p n (h c) -> p (n h) c", c=P), AX,
                                          ALU.add).then_inc(sub_sum, 1)
                        dve.wait_ge(sub_std, 1)
                        link(dve.reciprocal(st_o[:, :], st_o[:, :]))
                        dve.tensor_tensor(heads, heads, st_o[:, :].unsqueeze(2).broadcast_to([P, 32, P]),
                                          ALU.mult).then_inc(att["diff"]["otok_done"], 1)
                else:
                    sub = stage[:-4]
                    fill(stage, turned(stage, None if sub == "dsa" else cols[:, COL["subln"]:COL["subln"] + 1]))
                    for j in range(KT):
                        lo_ahead(stage, j)
                        dve.wait_ge(unit_done, UNIT_BASE[stage] + j + 1)
                        dve.tensor_copy(y_mix[:, j, :], bank[j % N_BANKS][:, :]).then_inc(bank_free[j % N_BANKS], 1)
                    post(sub)


def units_of(w):
    k, n = w.shape
    return np.ascontiguousarray(w.reshape(k // P, P, n // P, P).transpose(2, 1, 0, 3).reshape(n // P, P, k))


def columns(v):
    return np.ascontiguousarray(v.reshape(-1, P).T)


def lay_out(i):
    f32 = np.float32
    w_in = i["w_in"][0]
    w_in = np.concatenate([w_in, np.zeros((D, len(IN_KINDS) * P - w_in.shape[1]), f32)], axis=1)
    up, down = [], []
    for layer in range(N_LAYERS):
        for s in range(2):
            pad = np.zeros((D, FT * P - F_FF), f32)
            g = units_of(np.concatenate([i["ffn_w_gate_2"][layer, s], pad], axis=1))
            u = units_of(np.concatenate([i["ffn_w_up_2"][layer, s], pad], axis=1))
            up.append(np.stack([g, u], axis=1).reshape(2 * FT, P, D))
            dn = units_of(np.concatenate([i["ffn_w_down_2"][layer, s], pad.T], axis=0))
            down.append(dn.reshape(KT, P, 2, FH * P).transpose(0, 2, 1, 3).reshape(2 * KT, P, FH * P))
    w = i["dsa_w_in_2"][0]
    q, k, v, qi, ki, wi_ = np.split(w, np.cumsum([16 * HD, HD, HD, 8 * HD, HD]), axis=1)
    w_dsa = np.concatenate([q, k, k, v, wi_, np.zeros((D, P - HD - 8), f32), qi, ki, ki], axis=1)
    inv = np.zeros(P, f32)
    sign = np.zeros(P, f32)
    rot = HD // ROT_FRAC
    freq = (ROPE_THETA ** (-np.arange(0, rot, 2, dtype=f32) / rot)).astype(f32)
    for p in range(P):
        if p % HD < rot:
            inv[p] = freq[p % HD % (rot // 2)]
            sign[p] = -1.0 if p % HD < rot // 2 else 1.0
    fox_b = np.zeros((P, 1), f32)
    fox_b[0:8, 0] = i["fox_b_f"][0]
    cols = np.concatenate([
        columns(i["norm_g"][0]), columns(i["final_norm_g"]), columns(i["pre_norm_2"]), columns(i["post_norm_2"]),
        columns(i["ada_b_2"]), np.tile(i["hgrn_onorm_g"][0], 2)[:, None], i["diff_subln_2"][0][:, None],
        columns(i["hgrn_lb"][0]), inv[:, None], sign[:, None], fox_b], axis=1).astype(f32)
    assert cols.shape == (P, N_COLS)
    key, query = np.arange(P)[:, None], np.arange(P)[None, :]
    level = np.zeros((P, 8, P), f32)
    for n in range(7):
        m = P >> (n + 1)
        level[:, n, :] = (key // (2 * m) == query // (2 * m)) & (key % (2 * m) < m) & (query % (2 * m) >= m)
    level[:, 7, :] = key == query
    keep = np.ones((P, SEQ), f32)
    keep[:, ::P] = 0.0
    return {
        "x": np.ascontiguousarray(i["x"][0].T), "cols": cols, "ident": np.eye(P, dtype=f32),
        "causal": np.where(query <= key, 0.0, NEG).astype(f32), "c": i["c_2"][0], "pos": i["positions_2"][0],
        "ws": np.ascontiguousarray(i["gmlp_w_s"][0].transpose(2, 0, 1)), "level": level, "keep": keep,
        "ln_g": i["gmlp_ln_g"][0].reshape(-1), "ln_b": i["gmlp_ln_b"][0].reshape(-1), "bs": i["gmlp_b_s"][0],
        "lam": i["diff_lambda_2"][0].reshape(-1),
        "ada": np.ascontiguousarray(i["ada_w_2"].transpose(0, 2, 1).reshape(2 * MOD_TILES, P, D)),
        "w_in": units_of(w_in), "w_out": units_of(i["w_out"][0]),
        "ffn_up": np.stack(up), "ffn_down": np.stack(down),
        "w_dsa": units_of(w_dsa), "w_dsa_out": units_of(i["dsa_w_out_2"][0]),
        "w_diff": units_of(i["diff_w_in_2"][0]), "w_diff_out": units_of(i["diff_w_out_2"][0]),
    }


def kernel(**inputs):
    import concourse.bacc as bacc
    from concourse.bass_utils import run_bass_kernel_spmd

    arrays = {f"in_{k}": np.ascontiguousarray(v) for k, v in lay_out({k: np.asarray(v) for k, v in inputs.items()}).items()}
    nc = bacc.Bacc("TRN2", target_bir_lowering=False, num_devices=1)
    A = {k[3:]: nc.dram_tensor(k, v.shape, mybir.dt.from_np(v.dtype), kind="ExternalInput").ap()
         for k, v in arrays.items()}
    out = nc.dram_tensor("out_0", (D, SEQ), F32, kind="ExternalOutput").ap()
    build(nc, A, out)
    r = run_bass_kernel_spmd(nc, [arrays], core_ids=[0])
    return np.ascontiguousarray(r.results[0]["out_0"].T)[None]
```

```python
from contextlib import ExitStack

import numpy as np

import concourse.bass as bass
from concourse import mybir

F32 = mybir.dt.float32
F32R = mybir.dt.float32r
BF16 = mybir.dt.bfloat16
U8 = mybir.dt.uint8
I32 = mybir.dt.int32
ALU = mybir.AluOpType
ACT = mybir.ActivationFunctionType
AX = mybir.AxisListType.X
ds = bass.ds

P = 128
SEQ = 512
D = 1024
KT = D // P
NT = SEQ // P
F_FF = 2752
FT = -(-F_FF // P)
FH = FT // 2
N_LAYERS = 2
MOD_TILES = 9 * D // P
HD = 64
EPS = 1e-6
F_FLOOR = 1e-30
NEG = -1.0e30
TAKEN = -3.0e38
TOPK = min(256, SEQ // 4)
N_RAW = 4
N_SPLIT = 2
WARM = (44, 40)
N_BANKS = 4
ROPE_THETA, ROT_FRAC = 500000.0, 4
LAM_INIT = 0.8 - 0.6 * float(np.exp(-0.3 * 1))

IN_KINDS = (["gelu"] * 2 + ["gelu_tok"] * 2 + ["silu"] * 2
            + ["silu"] * 2 + ["copy"] * 2 + ["tok"] * 2 + ["silu"] * 2
            + ["copy"] * 8 + ["tok"] * 4 + ["silu"] * 4 + ["copy"])
DSA_KINDS = ["tok"] + ["rope"] * 4 + ["rope"] + ["rope"] + ["rope"] * 8
DIFF_KINDS = ["rope"] * 16 + ["tok"] * 8

STAGE_UNITS = [("in", len(IN_KINDS)), ("out", KT),
               ("ffn0", 2 * FT + 2 * KT), ("dsa", len(DSA_KINDS)), ("dsa_out", KT), ("ffn1", 2 * FT + 2 * KT),
               ("ffn2", 2 * FT + 2 * KT), ("diff", len(DIFF_KINDS)), ("diff_out", KT), ("ffn3", 2 * FT + 2 * KT)]
STAGES = [name for name, _ in STAGE_UNITS]
UNIT_BASE = {n: sum(c for _, c in STAGE_UNITS[:i]) for i, n in enumerate(STAGES)}
FILL = {n: i for i, n in enumerate(STAGES)}

SUBS = ["ffn0", "dsa", "ffn1", "ffn2", "diff", "ffn3"]
PRE = {s: 2 + 2 * i for i, s in enumerate(SUBS)}
POST = {s: 3 + 2 * i for i, s in enumerate(SUBS)}
N_NORMS = 2 + 2 * len(SUBS)
ON_POOL = [n == 1 or n in POST.values() for n in range(N_NORMS)]
SUMS = [sum(9 if p_ else 8 for p_ in ON_POOL[:n]) for n in range(N_NORMS + 1)]

COL = {}
_at = 0
for _name, _n in (("norm_g", KT), ("final_g", KT), ("pre", 6 * KT), ("post", 6 * KT), ("ada_b", 2 * MOD_TILES),
                  ("onorm", 1), ("subln", 1), ("lb", 2), ("inv_freq", 1), ("sign", 1), ("fox_b", 1)):
    COL[_name] = _at
    _at += _n
N_COLS = _at


def bank_plan():
    uses, plan = [0] * N_BANKS, {}
    for name, n in STAGE_UNITS:
        if name.startswith("ffn"):
            plan[name, "up"] = list(uses)
            uses = [u + 2 * FT // N_BANKS for u in uses]
            plan[name, "down"] = list(uses)
            uses = [u + (KT // 2 if b < 2 else 0) for b, u in enumerate(uses)]
        else:
            plan[name, "all"] = list(uses)
            for j in range(n):
                uses[j % N_BANKS] += 1
    return plan


BANK_USES = bank_plan()
TOK = {"in": 0, "fox_out": 8, "dsa": 12, "dsa_out": 13, "diff": 21, "diff_out": 29}


class Chain:

    def __init__(self, eng, sem):
        self.eng, self.sem, self.n, self.per, self.it = eng, sem, 0, 0, None

    def link(self, ins):
        ins.then_inc(self.sem, 1)
        self.n += 1
        self.eng.wait_ge(self.sem, self.n if self.it is None else self.it * self.per + self.n)

    def body(self, it, per):
        self.it, self.per, self.start = it, per, self.n

    def leave(self, count):
        assert self.n - self.start == self.per, (self.n - self.start, self.per)
        self.it = None
        self.n = self.start + self.per * count


def build(nc, A, out, last="ffn3"):
    ctx = ExitStack()
    with ctx:
        place = {"at": 16512}

        def sb(name, shape, dt=F32, at=None):
            size = int(np.prod(shape[1:])) * mybir.dt.size(dt)
            if at is None:
                at = place["at"]
                place["at"] = at + -(-size // 32) * 32
            return nc.alloc_sbuf_tensor_at(name, shape, dt, offset=at)

        def sem(name):
            return ctx.enter_context(nc.semaphore(name))

        run = STAGES[:STAGES.index(last) + 1]
        n_units = UNIT_BASE[last] + dict(STAGE_UNITS)[last]

        x = sb("x", [P, KT, SEQ])
        H_AT = place["at"]
        h_hi = sb("h_hi", [P, KT, SEQ], F32R)
        h_lo = sb("h_lo", [P, KT, SEQ], F32R)
        y = sb("y", [P, KT, SEQ], at=H_AT)
        raw = [sb(f"raw{i}", [P, FH * P]) for i in range(N_RAW)]
        w_hi = [sb(f"w_hi{i}", [P, FH * P], F32R) for i in range(N_SPLIT)]
        w_lo = [sb(f"w_lo{i}", [P, FH * P], F32R) for i in range(N_SPLIT)]
        ada = [sb(f"ada{i}", [P, D]) for i in range(2)]
        cond = sb("cond", [P, D])
        sq = [sb(f"sq{i}", [P, SEQ]) for i in range(2)]
        acc = sb("acc", [P, SEQ])
        rstd = sb("rstd", [P, SEQ])
        t = [sb(f"t{i}", [P, SEQ]) for i in range(2)]
        cols = sb("cols", [P, N_COLS])
        mod_raw = sb("mod_raw", [P, 2 * MOD_TILES])
        gain = sb("gain", [P, 6 * KT])
        coef = sb("coef", [P, 6 * KT])
        ident = sb("ident", [P, P])
        ones = sb("ones", [P, P])
        consts_bf = sb("consts_bf", [P, 2 * P], BF16)
        ident_bf = consts_bf[:, 0:P]
        causal_bf = consts_bf[:, P:2 * P]
        eps_col = sb("eps_col", [P, 1])
        lam_col = sb("lam_col", [P, 4])
        BIG = place["at"]

        def big(name, at, shape, dt=F32):
            return sb(name, shape, dt, at=BIG + 4 * at)

        a_hi = big("a_hi", 0, [P, FT, SEQ], F32R)
        a_lo = big("a_lo", FT * SEQ, [P, FT, SEQ], F32R)

        au = big("au", 0, [P, 2, SEQ])
        av = big("av", 1024, [P, NT, 256])
        az = big("az", 2048, [P, 2, SEQ])
        bq = big("bq", 3072, [P, 2, SEQ])
        bf = big("bf", 4096, [P, 2, SEQ])
        bi = big("bi", 5120, [P, NT, 256])
        bz = big("bz", 6144, [P, 2, SEQ])
        cq = big("cq", 7168, [P, 4, SEQ])
        ck = big("ck", 9216, [P, 4, SEQ])
        cv = big("cv", 11264, [P, NT, 512])
        cz = big("cz", 13312, [P, 4, SEQ])
        cf = big("cf", 15360, [P, SEQ])
        ws = big("ws", 15872, [P, 4, P])
        bs_bc = big("bs_bc", 16384, [P, 2, P])
        ln_g = big("ln_g", 16640, [P, 256])
        ln_b = big("ln_b", 16896, [P, 256])
        st = big("st", 17152, [P, 4, 16])
        level = big("level", 17216, [P, 8, P], U8)
        level_raw = big("level_raw", 21056, [P, 8, P])
        keep = big("keep", 17472, [P, SEQ])[:, :]
        bk = big("bk", 17984, [P, 2, SEQ])
        bb = big("bb", 19008, [P, 2, SEQ])
        bt = big("bt", 20032, [P, 2, SEQ])
        bx = big("bx", 21056, [P, 2, SEQ])
        state = big("state", 22080, [P, 3, 2, HD])
        bcol = big("bcol", 22464, [P, 64])
        sc = big("sc", 0, [P, 4, SEQ])
        kh_tok = big("kh_tok", 2048, [P, NT, 256])
        nc_row = big("nc_row", 0, [P, 8, SEQ])
        block1 = dict(q=cq, k=ck, v=cv, P=big("fP", 4096, [P, 4, SEQ]), PT=big("fPT", 17984, [P, 2, SEQ]),
                      otok=big("fotok", 19008, [P, NT, 512]), qs=big("fqs", 21056, [P, 1, SEQ]), ks=big("fks", 6144, [P, 1, SEQ]),
                      st=big("fst", 21568, [P, 3, 16]), ot=big("fot", 21696, [P, P]))

        y_mix = big("y_mix", 0, [P, KT, SEQ])
        dq = big("dq", 0, [P, 8, SEQ])
        dk = big("dk", 4096, [P, SEQ])
        dv = big("dv", 4608, [P, NT, P])
        dqi = big("dqi", 5120, [P, 4, SEQ])
        dki = big("dki", 7168, [P, SEQ])
        dcos = big("dcos", 7680, [P, SEQ])
        dsin = big("dsin", 8192, [P, SEQ])
        dshuf = [big(f"dshuf{i}", 8704 + 512 * i, [P, SEQ]) for i in range(2)]
        rel = [big(f"rel{i}", 9728 + 512 * i, [P, SEQ]) for i in range(2)]
        score = [big(f"score{i}", 10752 + 512 * i, [P, SEQ]) for i in range(2)]
        top8 = big("top8", 11776, [P, 2, 8])
        wi = big("wi", 11840, [P, NT, 8])
        mask = big("mask", 12288, [P, NT, SEQ], BF16)
        dsa = dict(q=dq, k=dk, v=dv, P=big("dP", 13312, [P, 4, SEQ]), PT=big("dPT", 15360, [P, 2, SEQ]),
                   otok=big("dotok", 16384, [P, NT, D]), qs=big("dqs", 20480, [P, 1, SEQ]),
                   st=big("dst", 20992, [P, 3, 16]), ot=big("dot", 21120, [P, P]))

        fq = big("fq", 0, [P, 8, SEQ])
        fk = big("fk", 4096, [P, 8, SEQ])
        fv = big("fv", 8192, [P, NT, D])
        fcos = big("fcos", 12288, [P, SEQ])
        fsin = big("fsin", 12800, [P, SEQ])
        fshuf = [big(f"fshuf{i}", 13312 + 512 * i, [P, SEQ]) for i in range(2)]
        lam_in = big("lam_in", 14336, [P, 4, HD])
        st_o = big("st_o", 14848, [P, NT, 8])
        diff = dict(q=fq, k=fk, v=fv, P=big("gP", 15360, [P, 4, SEQ]), PT=big("gPT", 17408, [P, 2, SEQ]),
                    otok=big("gotok", 18432, [P, NT, D]), qs=big("gqs", 13312, [P, 2, SEQ]), ks=big("gks", 12288, [P, 2, SEQ]),
                    st=big("gst", 14656, [P, 3, 16]), ot=big("got", 14720, [P, P]))

        assert BIG + 2 * 4 * FT * SEQ <= 229344, BIG + 2 * 4 * FT * SEQ

        bank = [ctx.enter_context(nc.psum_tensor(f"bank{i}", [P, SEQ], F32)) for i in range(8)]

        raw_landed = [sem(f"raw_landed{i}") for i in range(N_RAW)]
        ada_landed = [sem(f"ada_landed{i}") for i in range(2)]
        hi_ready, lo_ready = sem("hi_ready"), sem("lo_ready")
        unit_done = sem("unit_done")
        bank_free = [sem(f"bank_free{i}") for i in range(N_BANKS)]
        ada_used = sem("ada_used")
        const_landed, c_landed = sem("const_landed"), sem("c_landed")
        x_landed = [sem(f"x_landed{d}") for d in range(KT)]
        b1_landed = sem("b1_landed")
        cond_ready, const_ready, ones_ready = sem("cond_ready"), sem("const_ready"), sem("ones_ready")
        sq_ready, sums_done, sqrt_done, rstd_ready = (
            sem("sq_ready"), sem("sums_done"), sem("sqrt_done"), sem("rstd_ready"))
        t_ready, hh_ready, hl_ready = sem("t_ready"), sem("hh_ready"), sem("hl_ready")
        u_ready, x_pool, x_odd, x_dve = sem("u_ready"), sem("x_pool"), sem("x_odd"), sem("x_dve")
        ahi_ready, alo_ready = sem("ahi_ready"), sem("alo_ready")
        tok_T, tok_done = sem("tok_T"), sem("tok_done")
        dve_step = sem("dve_step")
        out_landed = sem("out_landed")

        block = ctx.enter_context(nc.Block())

        def read_of(stage, j, it=0):
            if not stage.startswith("ffn"):
                b = j % N_BANKS
                uses = BANK_USES[stage, "all"][b] + j // N_BANKS
            elif j < 2 * FT:
                b = j % N_BANKS
                uses = BANK_USES[stage, "up"][b] + j // N_BANKS
            else:
                b = (j - 2 * FT) % 4 // 2
                uses = BANK_USES[stage, "down"][b] + (j - 2 * FT) // 4
            return bank_free[b], uses + 1 + it

        def in_dst(j):
            for buf, lo_, hi_ in ((au, 0, 2), (az, 4, 6), (bq, 6, 8), (bf, 8, 10), (bz, 12, 14), (cq, 14, 18),
                                  (ck, 18, 22), (cz, 26, 30)):
                if lo_ <= j < hi_:
                    return buf[:, j - lo_, :]
            return cf[:, :]

        def tok_dst(stage, j):
            if stage == "dsa":
                return dv[:, :, :]
            if stage == "diff":
                return fv[:, :, (j - 16) * P:(j - 15) * P]
            for buf, lo_, hi_ in ((av, 2, 4), (bi, 10, 12), (cv, 22, 26)):
                if lo_ <= j < hi_:
                    return buf[:, :, (j - lo_) * P:(j - lo_ + 1) * P]

        def rope_dst(stage, j):
            if stage == "diff":
                return fq[:, j, :] if j < 8 else fk[:, j - 8, :]
            return dqi[:, j - 1, :] if j < 5 else dki[:, :] if j == 5 else dk[:, :] if j == 6 else dq[:, j - 7, :]

        def y_of(sub):
            return y if sub.startswith("ffn") else y_mix

        def x_ready(i, d):
            return (x_dve, d + 1) if i < 0 else ((x_pool, x_odd)[d % 2], KT // 2 * i + d // 2 + 1)

        def ffn_no(stage):
            return int(stage[3])

        def mod_col(i, seg, d):
            at = i // 3 * MOD_TILES + (3 * (i % 3) + seg) * KT + d
            return mod_raw[:, at:at + 1]

        def shift_col(i, d):
            return mod_col(i, 0, d)

        ORDER = (2, 0, 3, 1)
        AHEAD = 3
        FOX_MAPS = DSA_MAPS = [(half, 0, qb) for half in range(2) for qb in ORDER]
        DIFF_MAPS = [(half, comp, qb) for half in range(2) for qb in ORDER for comp in range(2)]

        def later(maps, it, u):
            if u >= len(maps):
                return None if isinstance(it, int) else (it + 1, u - len(maps))
            return it, u

        ROT = {"dsa": 0, "diff": 14}
        IX_AT = {1: 7, 2: 9, 3: 11}
        TOP_AT = {7: (1, 0, 4), 8: (1, 4, 16), 9: (2, 0, 3), 10: (2, 3, 16), 11: (3, 0, 2), 12: (3, 2, 7),
                  13: (3, 7, 12), 14: (3, 12, 16)}

        TOK_DONE = {"in": 0, "dsa": 8, "diff": 9}

        def raw_width(stage, j):
            return FH * P if stage.startswith("ffn") and j >= 2 * FT else D

        def unit_stage(g):
            for s in reversed(STAGES):
                if g >= UNIT_BASE[s]:
                    return s

        def width_of(g):
            s = unit_stage(g)
            return raw_width(s, g - UNIT_BASE[s])

        names = ("qs_ready", "s_ready", "nm_ready", "p_ready", "tr_ready", "pt_act", "pt_dve", "o_ready", "o_read",
                 "otok_done")
        att = {k: {n: sem(f"{k}_{n}") for n in names} for k in ("fox", "dsa", "diff")}
        rope = {k: {n: sem(f"{k}_{n}") for n in ("pos_landed", "angle", "table")} for k in ("dsa", "diff")}
        shuffled, rot_step, rotated = sem("shuffled"), sem("rot_step"), sem("rotated")
        fox_c_ready, fox_c_landed = sem("fox_c_ready"), sem("fox_c_landed")
        b1 = {n: sem(f"b1_{n}") for n in (
            "ws", "var", "std", "vn", "mixed", "lb", "lb_exp", "exps", "f", "ln", "b", "e_in", "e_out", "kh", "kh_T",
            "kh_tok", "kv", "state", "x", "levels", "copied", "sc", "o", "osq", "oss", "ostd", "c_in", "c_out",
            "bd")}
        ix = {n: sem(f"ix_{n}") for n in ("logit", "relu", "read", "mask")}
        lam_landed, lam_sum, lam_exp = sem("lam_landed"), sem("lam_sum"), sem("lam_exp")
        sub_inv, sub_std = sem("sub_inv"), sem("sub_std")
        last_sub = sum(1 for n in SUBS if (n if n.startswith("ffn") else n + "_out") in run) - 1

        def ada_of(stage, j):
            n0 = MOD_TILES
            if stage == "in":
                return [0, 1] if j == 0 else [j + 1]
            if stage == "out":
                return [n0 - KT + j]
            if stage == "ffn0":
                return [n0 + j]
            if stage == "ffn1" and j < 2 * MOD_TILES - n0 - (2 * FT + 2 * KT):
                return [n0 + 2 * FT + 2 * KT + j]
            return []

        ADA_FOX = len(IN_KINDS) + 1
        assert ADA_FOX + len(FOX_MAPS) * 4 == MOD_TILES - KT and len(FOX_MAPS) % 2 == 0
        ADA_FFN1 = (MOD_TILES - (2 * FT + 2 * KT)) // 4
        assert MOD_TILES - (2 * FT + 2 * KT) == 4 * ADA_FFN1

        def loops(stage):
            up, down = 2 * FT // 4, 2 * KT // 4
            if stage == "ffn0":
                return [(0, up, 1, "up"), (2 * FT, down, 1, "down")]
            if stage == "ffn1":
                return [(0, ADA_FFN1, 1, "up"), (4 * ADA_FFN1, up - ADA_FFN1, 0, "up"), (2 * FT, down, 0, "down")]
            return [(0, up, 0, "up"), (2 * FT, down, 0, "down")]

        def bodies(eng, count, body, chain=None, per=0):
            with eng.Fori(0, count - 1) as it:
                if chain:
                    chain.body(it, per)
                body(it)
            if chain:
                chain.leave(count - 1)
            body(count - 1)

        def ada_index(stage, first, j, it):
            base = MOD_TILES if stage == "ffn0" else MOD_TILES + 2 * FT + 2 * KT
            return base + first + j + 4 * it

        def subln(eng, tiles):
            heads = diff["otok"][:, tiles, :].rearrange("p n (h c) -> p (n h) c", c=P)
            scale = st_o[:, tiles, :].rearrange("p n h -> p (n h)")
            eng.tensor_tensor(heads, heads, scale.unsqueeze(2).broadcast_to([P, 8 * (tiles.stop - tiles.start), P]),
                              ALU.mult).then_inc(att["diff"]["otok_done"], 1)

        @block.sync
        def _(sp):
            for d in range(KT):
                sp.dma_start(x[:, d, :], A["x"][d * P:(d + 1) * P, :]).then_inc(x_landed[d], 16)
            sp.dma_start(cols[:, :], A["cols"]).then_inc(const_landed, 16)
            sp.dma_start(ident[:, :], A["ident"]).then_inc(const_landed, 16)
            sp.dma_start(t[0][:, 0:P], A["causal"]).then_inc(const_landed, 16)
            sp.dma_start(cond[:, :], A["c"].partition_broadcast(P)).then_inc(c_landed, 16)

            def load_unit(stage, j, it=0):
                g = UNIT_BASE[stage] + j
                slot, w = g % N_RAW, raw_width(stage, j)
                if g >= N_RAW:
                    sp.wait_ge(lo_ready, g - N_RAW + 1 + 4 * it)
                if stage.startswith("ffn"):
                    n = int(stage[3])
                    if j < 2 * FT:
                        src = A["ffn_up"][n, ds(j + 4 * it, 1)]
                    else:
                        src = A["ffn_down"][n, ds(j - 2 * FT + 4 * it, 1)]
                    src = src.rearrange("a p n -> (a p) n")
                else:
                    src = A["w_" + stage][j]
                sp.dma_start(raw[slot][:, 0:w], src).then_inc(raw_landed[slot], 16)

            for stage in run:
                if stage == "in":
                    for j in range(len(IN_KINDS)):
                        load_unit(stage, j)
                        if j == 2:
                            b1 = [(ws[:, :, :], A["ws"]), (level_raw[:, :, :], A["level"]), (keep, A["keep"]),
                                  (ln_g[:, :], A["ln_g"].partition_broadcast(P)),
                                  (ln_b[:, :], A["ln_b"].partition_broadcast(P))]
                            for g in range(4):
                                b1.append((bs_bc[g % 2 * HD:g % 2 * HD + HD, g // 2, :],
                                           A["bs"][g].partition_broadcast(HD)))
                            for dst, src in b1:
                                sp.dma_start(dst, src).then_inc(b1_landed, 16)
                elif stage.startswith("ffn"):
                    for first, count, _ada, _part in loops(stage):
                        with sp.Fori(0, count) as it:
                            for j in range(4):
                                load_unit(stage, first + j, it)
                else:
                    for j in range(dict(STAGE_UNITS)[stage]):
                        load_unit(stage, j)

            for d in range(KT):
                sp.wait_ge(*x_ready(last_sub, d))
                sp.dma_start(out[d * P:(d + 1) * P, :], x[:, d, :]).then_inc(out_landed, 16)
            sp.wait_ge(out_landed, 16 * KT)

        @block.scalar
        def _(act):
            def hi(g, w, it=0):
                act.wait_ge(raw_landed[g % N_RAW], 16 * (g // N_RAW + 1) + 16 * it)
                if g >= N_SPLIT:
                    act.wait_ge(unit_done, g - N_SPLIT + 1 + 4 * it)
                act.activation(w_hi[g % N_SPLIT][:, 0:w], raw[g % N_RAW][:, 0:w], ACT.Copy).then_inc(hi_ready, 1)

            def hi_ahead(stage, j, it=0):
                g = UNIT_BASE[stage] + j + N_SPLIT
                if not isinstance(it, int):
                    hi(g, raw_width(stage, j), it)
                elif g + 4 * it < n_units:
                    hi(g, width_of(g + 4 * it), it)

            def square(n, d, src):
                if n or d >= 2:
                    act.wait_ge(sums_done, SUMS[n] + (d - 1 + ON_POOL[n] if d >= 2 else 0))
                act.activation(sq[d % 2][:, :], src, ACT.Square).then_inc(sq_ready, 1)

            def std(n):
                act.wait_ge(sums_done, SUMS[n + 1])
                act.activation(rstd[:, :], bank[6][:, :], ACT.Sqrt, bias=eps_col[:, 0:1],
                               scale=1.0 / D).then_inc(sqrt_done, 1)

            def fill_hi(stage, d, bias=None):
                if d == 0:
                    act.wait_ge(unit_done, UNIT_BASE[stage])
                act.wait_ge(t_ready, 8 * FILL[stage] + d + 1)
                if bias is None:
                    ins = act.activation(h_hi[:, d, :], t[d % 2][:, :], ACT.Copy)
                else:
                    ins = act.activation(h_hi[:, d, :], t[d % 2][:, :], ACT.Identity, bias=bias)
                ins.then_inc(hh_ready, 1)


            def pre(stage):
                i = SUBS.index(stage)
                for d in range(KT):
                    act.wait_ge(*x_ready(i - 1, d))
                    square(PRE[stage], d, x[:, d, :])
                std(PRE[stage])
                for d in range(KT):
                    fill_hi(stage, d, shift_col(i, d))

            def y_square(sub, stage, j, d):
                act.wait_ge(*read_of(stage, j))
                square(POST[sub], d, y_mix[:, d, :])

            def ffn(stage):
                pre(stage)
                for first, count, _ada, part in loops(stage):
                    def up(it):
                        for f in range(2):
                            j = first + 2 * f
                            hi_ahead(stage, j, it)
                            act.wait_ge(unit_done, UNIT_BASE[stage] + j + 1 + 4 * it)
                            act.activation(sq[f][:, :], bank[2 * f][:, :], ACT.Silu).then_inc(bank_free[2 * f], 1)
                            hi_ahead(stage, j + 1, it)
                            act.wait_ge(*read_of(stage, j + 1, it))
                            act.activation(a_hi[:, ds(first // 2 + f + 2 * it, 1), :].rearrange("p a n -> p (a n)"),
                                           t[f][:, :], ACT.Copy).then_inc(ahi_ready, 1)

                    def down(it):
                        for d in range(2):
                            j = first + 2 * d
                            hi_ahead(stage, j, it)
                            hi_ahead(stage, j + 1, it)
                            act.wait_ge(unit_done, UNIT_BASE[stage] + j + 2 + 4 * it)
                            act.wait_ge(sums_done, SUMS[POST[stage]] + d + 2 * it)
                            act.activation(sq[d][:, :], bank[d][:, :], ACT.Square).then_inc(sq_ready, 1)
                    bodies(act, count, up if part == "up" else down)
                std(POST[stage])

            def evac_unit(stage, j, func, dst):
                act.wait_ge(unit_done, UNIT_BASE[stage] + j + 1)
                return act.activation(dst, bank[j % N_BANKS][:, :], func)

            def attend(k, cfg, maps, rounds):
                s = att[k]
                B = len(maps)

                def exp(it, u):
                    w = (maps[u][2] + 1) * P
                    act.wait_ge(s["nm_ready"], B * it + u + 1)
                    if u >= 4 or (u < 2 and not isinstance(it, int)):
                        act.wait_ge(s["tr_ready"], B * it + u - 3)
                    act.activation(cfg["P"][:, u % 4, 0:w], bank[u % 4][:, 0:w], ACT.Exp,
                                   bias=cfg["st"][:, 0, u:u + 1],
                                   accum_out=cfg["st"][:, 1, u:u + 1]).then_inc(s["p_ready"], 1)

                def body(it):
                    for u in range(B):
                        if u % 2 == 0:
                            w = (maps[u][2] + 1) * P
                            act.wait_ge(s["tr_ready"], B * it + u + 1)
                            if u >= 2:
                                act.wait_ge(s["o_ready"], B * it + u - 1)
                            act.activation(cfg["PT"][:, 0, 0:w], bank[4][:, 0:w], ACT.Copy).then_inc(s["pt_act"], 1)
                        if later(maps, it, u + 2):
                            exp(*later(maps, it, u + 2))
                exp(0, 0)
                exp(0, 1)
                bodies(act, rounds, body)

            def level_exp(i):
                act.wait_ge(b1["e_in"], i + 1)
                buf = bx if i % 2 == 0 else bf
                act.activation(buf[:, :, :], buf[:, :, :], ACT.Exp).then_inc(b1["e_out"], 1)

            def relu(qb):
                w = (qb + 1) * P
                for h in range(8):
                    n = 8 * (qb - 1) + h
                    act.wait_ge(ix["logit"], n + 1)
                    if n >= 2:
                        act.wait_ge(ix["read"], n - 1)
                    act.activation(rel[n % 2][:, 0:w], bank[4 + n % 4][:, 0:w], ACT.Relu).then_inc(ix["relu"], 1)

            def beside_in(j):
                if j == 8:
                    act.wait_ge(b1["var"], 1)
                    act.activation(st[:, 3, :], st[:, 2, :], ACT.Sqrt, bias=eps_col[:, 0:1],
                                   scale=1.0 / HD).then_inc(b1["std"], 1)
                elif j == 12:
                    act.wait_ge(b1["lb"], 1)
                    act.activation(bcol[:, 2:4], bcol[:, 0:2], ACT.Exp).then_inc(b1["lb_exp"], 1)
                    act.wait_ge(*read_of("in", 9))
                    act.wait_ge(*read_of("in", 8))
                    act.activation(bk[:, :, :], bf[:, :, :], ACT.Exp).then_inc(b1["exps"], 1)
                    act.activation(bt[:, :, :], bf[:, :, :], ACT.Exp, scale=-1.0).then_inc(b1["exps"], 1)
                elif j == 22:
                    act.wait_ge(b1["f"], 1)
                    act.activation(bf[:, :, :], bf[:, :, :], ACT.Ln).then_inc(b1["ln"], 1)
                elif j == 26:
                    act.wait_ge(b1["b"], 1)
                    act.activation(bt[:, :, :], bb[:, :, :], ACT.Exp).then_inc(b1["e_out"], 1)
                    act.activation(bcol[:, 8:16].rearrange("p (a n) -> p a n", a=2),
                                   bb[:, :, :].rearrange("p a (n s) -> p a n s", s=P)[:, :, :, P - 1],
                                   ACT.Exp).then_inc(b1["e_out"], 1)
                    level_exp(0)
                elif j == 29:
                    level_exp(1)

            def block1_mixers():
                for d in (0, 1):
                    fill_hi("out", d)
                level_exp(2)
                act.wait_ge(b1["c_in"], 1)
                act.activation(t[0][0:8, :], t[0][0:8, :], ACT.Exp).then_inc(b1["c_out"], 1)
                act.wait_ge(b1["c_in"], 2)
                act.activation(t[0][0:8, :], t[0][0:8, :], ACT.Ln).then_inc(b1["c_out"], 1)
                for i in range(3, 8):
                    level_exp(i)
                for a in range(2):
                    act.wait_ge(b1["o"], a + 1)
                    act.activation(bx[:, a, :], bank[4 + a][:, :], ACT.Square).then_inc(b1["osq"], 1)
                act.wait_ge(fox_c_ready, 1)
                act.dma_start(nc_row[0:1, :, :], cf[0:8, :]).then_inc(fox_c_landed, 16)
                for a in range(2):
                    act.wait_ge(b1["oss"], a + 1)
                    act.activation(bt[:, a, :], bank[6 + a][:, :], ACT.Sqrt, bias=eps_col[:, 0:1],
                                   scale=1.0 / HD).then_inc(b1["ostd"], 1)
                for d in (2, 3):
                    fill_hi("out", d)
                attend("fox", block1, FOX_MAPS, 4)
                for d in range(4, 8):
                    fill_hi("out", d)

            for stage in run:
                if stage == "in":
                    for d in range(KT):
                        act.wait_ge(x_landed[d], 16)
                        square(0, d, x[:, d, :])
                        if d in (4, 6):
                            hi((d - 4) // 2, D)
                    act.wait_ge(const_ready, 1)
                    std(0)
                    for d in range(KT):
                        fill_hi(stage, d)
                    act.wait_ge(c_landed, 16)
                    act.activation(cond[:, :], cond[:, :], ACT.Silu).then_inc(cond_ready, 1)
                    m = 0
                    for j, kind in enumerate(IN_KINDS):
                        hi_ahead(stage, j)
                        if kind == "gelu_tok":
                            if m >= 2:
                                act.wait_ge(tok_T, m - 1)
                            evac_unit(stage, j, ACT.Gelu_apprx_tanh, sq[m % 2][:, :]).then_inc(bank_free[j % N_BANKS], 1)
                        elif kind in ("gelu", "silu"):
                            evac_unit(stage, j, ACT.Gelu_apprx_tanh if kind == "gelu" else ACT.Silu,
                                      in_dst(j)).then_inc(bank_free[j % N_BANKS], 1)
                        m += kind.endswith("tok")
                        beside_in(j)
                elif stage == "out":
                    block1_mixers()
                    for j in range(KT):
                        hi_ahead(stage, j)
                        act.wait_ge(*read_of(stage, j))
                        square(1, j, x[:, j, :])
                    std(1)
                elif stage.startswith("ffn"):
                    ffn(stage)
                elif stage in ("dsa", "diff"):
                    kinds = DSA_KINDS if stage == "dsa" else DIFF_KINDS
                    act.wait_ge(unit_done, UNIT_BASE[stage])
                    dst = {"dsa": dshuf[0], "diff": fshuf[0]}[stage]
                    act.dma_start(dst[:, :].bitcast(I32), A["pos"].partition_broadcast(P)).then_inc(
                        rope[stage]["pos_landed"], 16)
                    if stage == "diff":
                        act.dma_start(lam_in[:, :, :].rearrange("p a b -> p (a b)"),
                                      A["lam"].partition_broadcast(P)).then_inc(lam_landed, 16)
                    pre(stage)
                    r = rope[stage]
                    cs, sn, sh = (dcos, dsin, dshuf) if stage == "dsa" else (fcos, fsin, fshuf)
                    act.wait_ge(r["angle"], 1)
                    act.activation(sn[:, :], sn[:, :], ACT.Sin).then_inc(r["table"], 1)
                    act.wait_ge(r["angle"], 2)
                    act.activation(cs[:, :], cs[:, :], ACT.Sin).then_inc(r["table"], 1)
                    for j, kind in enumerate(kinds):
                        hi_ahead(stage, j)
                        if kind == "rope":
                            act.wait_ge(unit_done, UNIT_BASE[stage] + j + 1)
                            act.activation(rope_dst(stage, j), bank[j % N_BANKS][:, :], ACT.Copy).then_inc(bank_free[j % N_BANKS], 1)
                        for qb in range(1, NT):
                            if stage == "dsa" and IX_AT[qb] == j:
                                relu(qb)
                    if stage == "dsa":
                        attend("dsa", dsa, DSA_MAPS, 8)
                    else:
                        act.wait_ge(lam_sum, 1)
                        act.activation(lam_col[:, 0:2], lam_col[:, 0:2], ACT.Exp).then_inc(lam_exp, 1)
                        attend("diff", diff, DIFF_MAPS, 4)
                        act.wait_ge(att["diff"]["otok_done"], 1)
                        act.activation(st_o[:, :, :], st_o[:, :, :], ACT.Sqrt, bias=eps_col[:, 0:1],
                                       scale=1.0 / P).then_inc(sub_std, 1)
                else:
                    sub = stage[:-4]
                    for d in range(KT):
                        fill_hi(stage, d)
                    for j in range(KT):
                        hi_ahead(stage, j)
                        y_square(sub, stage, j, j)
                    std(POST[sub])

        @block.tensor
        def _(pe):
            def open_unit(stage, j, b, uses, it=0):
                pe.wait_ge(lo_ready, UNIT_BASE[stage] + j + 1 + 4 * it)
                if uses is not None and (not isinstance(it, int) or uses + it > 0):
                    pe.wait_ge(bank_free[b], uses + it)

            def products(stage, j, b, k, kx, start, stop, rhs=(h_hi, h_lo)):
                slot = (UNIT_BASE[stage] + j) % N_SPLIT
                hi_, lo_ = w_hi[slot][:, k * P:(k + 1) * P], w_lo[slot][:, k * P:(k + 1) * P]
                pe.matmul(bank[b][:, :], hi_, rhs[0][:, kx, :], start=start, stop=False)
                pe.matmul(bank[b][:, :], hi_, rhs[1][:, kx, :], start=False, stop=False)
                return pe.matmul(bank[b][:, :], lo_, rhs[0][:, kx, :], start=False, stop=stop)

            def unit(stage, j, b, uses, k0=0, nk=KT, start=True, stop=True, it=0, rhs=(h_hi, h_lo)):
                open_unit(stage, j, b, uses if start else None, it)
                for k in range(nk):
                    mm = products(stage, j, b, k, k0 + k, start and k == 0, stop and k == nk - 1, rhs)
                mm.then_inc(unit_done, 1)

            def first_units(stage, uses):
                lag = 3
                open_unit(stage, 0, 0, uses[0])
                for k in range(KT + lag):
                    if k < KT:
                        pe.wait_ge(hl_ready, KT * FILL[stage] + k + 1)
                        mm = products(stage, 0, 0, k, k, k == 0, k == KT - 1)
                        if k == KT - 1:
                            mm.then_inc(unit_done, 1)
                    if k == lag:
                        open_unit(stage, 1, 1, uses[1])
                    if k >= lag:
                        mm = products(stage, 1, 1, k - lag, k - lag, k == lag, k == KT + lag - 1)
                mm.then_inc(unit_done, 1)

            def projected(stage, j):
                if j == 0:
                    first_units(stage, BANK_USES[stage, "all"])
                elif j >= 2:
                    unit(stage, j, j % N_BANKS, BANK_USES[stage, "all"][j % N_BANKS] + j // N_BANKS)

            def keep_warm(count):
                for _ in range(count):
                    pe.matmul(bank[7][:, 0:2 * P], ident_bf[:, :], consts_bf[:, :], start=True, stop=True)

            def total(n):
                pe.wait_ge(rstd_ready, n)
                pe.wait_ge(sums_done, SUMS[n] + KT)
                pe.matmul(bank[6][:, :], ones[:, :], acc[:, :], start=True, stop=False)
                pe.wait_ge(sq_ready, KT * (n + 1))
                pe.matmul(bank[6][:, :], ones[:, :], sq[(KT - 1) % 2][:, :], start=False,
                          stop=True).then_inc(sums_done, 1)
                if n < N_NORMS - 1:
                    keep_warm(WARM[0])

            def sum_squares(n):
                if n:
                    pe.wait_ge(rstd_ready, n)
                for d in range(KT):
                    pe.wait_ge(sq_ready, KT * n + d + 1)
                    pe.matmul(bank[6][:, :], ones[:, :], sq[d % 2][:, :], start=d == 0,
                              stop=d == KT - 1).then_inc(sums_done, 1)
                if n:
                    keep_warm(WARM[1])

            def four_transposes(m, src):
                for n in range(NT):
                    mm = pe.transpose(bank[4 + m % 2][:, n * P:(n + 1) * P], src(n), ident[:, :])
                mm.then_inc(tok_T, 1)

            def projections(stage, kinds):
                m = TOK[stage]
                pending = None

                def flush():
                    m, j = pending
                    pe.wait_ge(*read_of(stage, j))
                    done = m - TOK[stage]
                    if done >= 2:
                        pe.wait_ge(tok_done, TOK_DONE[stage] + done - 1)
                    four_transposes(m, lambda n: sq[m % 2][:, n * P:(n + 1) * P])

                for j, kind in enumerate(kinds):
                    projected(stage, j)
                    if pending is not None:
                        flush()
                        pending = None
                    if kind.endswith("tok"):
                        pending = (m, j)
                        m += 1
                    if stage == "in":
                        beside_in(j)
                    for qb in range(1, NT):
                        if stage == "dsa" and IX_AT[qb] == j:
                            logits(qb)
                if pending is not None:
                    flush()

            def logits(qb):
                pe.wait_ge(rotated, ROT["dsa"] + 5)
                w = (qb + 1) * P
                for h in range(8):
                    n = 8 * (qb - 1) + h
                    r = slice(h % 2 * HD, h % 2 * HD + HD)
                    if n >= 4:
                        pe.wait_ge(ix["relu"], n - 3)
                    pe.matmul(bank[4 + n % 4][:, 0:w], dqi[r, h // 2, qb * P:(qb + 1) * P], dki[r, 0:w],
                              start=True, stop=True).then_inc(ix["logit"], 1)

            def attend(k, cfg, maps, rounds):
                s = att[k]
                B = len(maps)

                def scores(it, u):
                    half, comp, qb = maps[u]
                    w = (qb + 1) * P
                    rows = slice(half * HD, half * HD + HD)
                    if u == 0:
                        pe.wait_ge(s["qs_ready"], it + 1)
                    if u >= 4 or (u < AHEAD and not isinstance(it, int)):
                        pe.wait_ge(s["p_ready"], B * it + u - 3)
                    if k == "dsa":
                        keys = cfg["k"][rows, 0:w]
                    else:
                        keys = cfg["ks"][rows, comp, 0:w]
                    out_ = bank[u % 4]
                    pe.matmul(out_[:, 0:w], cfg["qs"][rows, comp, qb * P:(qb + 1) * P], keys,
                              start=True, stop=False)
                    if k == "fox":
                        pe.matmul(out_[:, 0:w], ones[0:1, :],
                                  nc_row[0:1, ds(2 * it + half, 1), 0:w].rearrange("p a n -> p (a n)"),
                                  start=False, stop=False)
                    if k == "dsa":
                        mm = pe.matmul(out_[:, 0:w], ident_bf[:, :], mask[:, qb, 0:w], start=False, stop=True)
                    else:
                        mm = pe.matmul(out_[:, qb * P:w], ident_bf[:, :], causal_bf[:, :], start=False, stop=True)
                    mm.then_inc(s["s_ready"], 1)

                def transposes(it, u):
                    qb = maps[u][2]
                    pe.wait_ge(s["p_ready"], B * it + u + 1)
                    for sblk in range(qb + 1):
                        mm = pe.transpose(bank[4 + u % 2][:, sblk * P:(sblk + 1) * P],
                                          cfg["P"][:, u % 4, sblk * P:(sblk + 1) * P], ident[:, :])
                    mm.then_inc(s["tr_ready"], 1)

                def values(it, u):
                    half, comp, qb = maps[u]
                    pe.wait_ge(s["pt_act" if u % 2 == 0 else "pt_dve"], (B // 2) * it + u // 2 + 1)
                    pe.wait_ge(s["o_read"], 2 + (B // 2 * it + u // 2 - 1 if k == "diff" else B * it + u - 1))
                    out_ = bank[6 + u // 2 % 2][:, comp * P:comp * P + P] if k == "diff" else bank[6 + u % 2][:, 0:HD]
                    for sblk in range(qb + 1):
                        if k == "dsa":
                            v = cfg["v"][:, sblk, 0:HD]
                        elif k == "fox":
                            v = cfg["v"][:, sblk, ds(it * P + half * HD, HD)]
                        else:
                            v = cfg["v"][:, sblk, ds(it * 2 * P + half * P, P)]
                        mm = pe.matmul(out_, cfg["PT"][:, u % 2, sblk * P:(sblk + 1) * P], v,
                                       start=sblk == 0, stop=sblk == qb)
                    mm.then_inc(s["o_ready"], 1)

                def body(it):
                    for u in range(B):
                        transposes(it, u)
                        if u:
                            values(it, u - 1)
                        if later(maps, it, u + AHEAD):
                            scores(*later(maps, it, u + AHEAD))
                    values(it, B - 1)

                for u in range(AHEAD):
                    scores(0, u)
                bodies(pe, rounds, body)

            def turn_back(stage, otok, count, d0=0):
                m0 = TOK[stage]
                for ft in range(count):
                    if ft >= 2:
                        pe.wait_ge(t_ready, 8 * FILL[stage if stage != "fox_out" else "out"] + d0 + ft - 1)
                    four_transposes(m0 + ft, lambda n: otok[:, n, ft * P:(ft + 1) * P])

            def beside_in(j):
                if j == 10:
                    pe.wait_ge(b1["ws"], 1)
                    pe.wait_ge(b1["vn"], 1)
                    for g in range(4):
                        for n in range(NT):
                            mm = pe.matmul(bank[6 + g // 2][g % 2 * HD:g % 2 * HD + HD, n * P:(n + 1) * P],
                                           av[:, n, g * HD:(g + 1) * HD], ws[:, g, :], start=True, stop=True)
                    mm.then_inc(b1["mixed"], 1)
                elif j == 29:
                    pe.wait_ge(b1["kh"], 1)
                    for a in range(2):
                        for n in range(NT):
                            mm = pe.transpose(bank[4 + a][:, n * P:(n + 1) * P], bx[:, a, n * P:(n + 1) * P], ident[:, :])
                        mm.then_inc(b1["kh_T"], 1)

            def block1_mixers():
                pe.wait_ge(b1["kh_tok"], 2)
                for n in range(3):
                    for h in range(4):
                        r = slice(h % 2 * HD, h % 2 * HD + HD)
                        c = (n * 2 + h // 2) * HD
                        mm = pe.matmul(bank[6][r, c:c + HD], kh_tok[:, n, h * HD:(h + 1) * HD],
                                       bi[:, n, h * HD:(h + 1) * HD], start=True, stop=True)
                mm.then_inc(b1["kv"], 1)
                for i in range(8):
                    if i < 7:
                        pe.wait_ge(b1["x"], i + 1)
                        keys = queries = bf if i % 2 == 0 else bx
                    else:
                        keys, queries = bk, bq
                    for h in range(4):
                        r = slice(h % 2 * HD, h % 2 * HD + HD)
                        if i:
                            pe.wait_ge(b1["copied"], 4 * (i - 1) + h + 1)
                        for n in range(NT):
                            c = slice(n * P, (n + 1) * P)
                            mm = pe.matmul(bank[h][:, c], keys[r, h // 2, c], queries[r, h // 2, c],
                                           start=True, stop=True)
                        mm.then_inc(b1["levels"], 1)
                pe.wait_ge(b1["copied"], 32)
                pe.wait_ge(b1["state"], 1)
                for a in range(2):
                    for h in (2 * a, 2 * a + 1):
                        r = slice(h % 2 * HD, h % 2 * HD + HD)
                        for n in range(NT):
                            c = slice(n * P, (n + 1) * P)
                            mm = pe.matmul(bank[4 + a][r, c], bi[:, n, h * HD:(h + 1) * HD], sc[:, h, c],
                                           start=True, stop=n == 0)
                            if n:
                                mm = pe.matmul(bank[4 + a][r, c], state[r, n - 1, a, :], bt[r, a, c],
                                               start=False, stop=True)
                    mm.then_inc(b1["o"], 1)
                pe.wait_ge(b1["bd"], 1)
                for a in range(2):
                    pe.wait_ge(b1["osq"], a + 1)
                    pe.matmul(bank[6 + a][:, :], ws[:, 0, :], bx[:, a, :], start=True, stop=True).then_inc(b1["oss"], 1)
                pe.wait_ge(fox_c_landed, 16)
                pe.wait_ge(hl_ready, 8 * FILL["out"] + 4)
                attend("fox", block1, FOX_MAPS, 4)
                pe.wait_ge(att["fox"]["otok_done"], 1)
                turn_back("fox_out", block1["otok"], 4, d0=4)

            pe.wait_ge(ones_ready, 1)
            for stage in run:
                if stage == "in":
                    sum_squares(0)
                    pe.wait_ge(const_ready, 1)
                    projections(stage, IN_KINDS)
                elif stage == "out":
                    block1_mixers()
                    for j in range(KT):
                        projected(stage, j)
                    total(1)
                elif stage.startswith("ffn"):
                    sum_squares(PRE[stage])
                    first_units(stage, BANK_USES[stage, "up"])
                    for j in (2, 3):
                        unit(stage, j, j, BANK_USES[stage, "up"][j])
                    with pe.Fori(1, 2 * FT // 4) as it:
                        for j in range(4):
                            unit(stage, j, j, BANK_USES[stage, "up"][j], it=it)
                    with pe.Fori(0, 2 * KT // 4) as it:
                        for j in range(4):
                            pe.wait_ge(alo_ready, FT * ffn_no(stage) + FH * (j % 2 + 1))
                            unit(stage, 2 * FT + j, j // 2, BANK_USES[stage, "down"][j // 2], k0=FH * (j % 2), nk=FH,
                                 start=j % 2 == 0, stop=j % 2 == 1, it=it, rhs=(a_hi, a_lo))
                    total(POST[stage])
                elif stage in ("dsa", "diff"):
                    sum_squares(PRE[stage])
                    projections(stage, DSA_KINDS if stage == "dsa" else DIFF_KINDS)
                    if stage == "dsa":
                        pe.wait_ge(rotated, ROT["dsa"] + 6)
                        pe.wait_ge(ix["mask"], 1)
                        attend("dsa", dsa, DSA_MAPS, 8)
                    else:
                        attend("diff", diff, DIFF_MAPS, 4)
                else:
                    sub = stage[:-4]
                    otok = (dsa if sub == "dsa" else diff)["otok"]
                    pe.wait_ge(att[sub]["otok_done"], 1 if sub == "dsa" else 3)
                    turn_back(stage, otok, KT)
                    for j in range(KT):
                        projected(stage, j)
                    total(POST[sub])

        @block.gpsimd
        def _(pool):
            def add_square(n, d, it_d=0):
                pool.wait_ge(sq_ready, 8 * n + d + 1 + it_d)
                pool.wait_ge(sums_done, SUMS[n] + d + 1 + it_d)
                pool.tensor_tensor(acc[:, :], acc[:, :], sq[d % 2][:, :], ALU.add).then_inc(sums_done, 1)

            def clear(n):
                pool.wait_ge(sums_done, SUMS[n])
                pool.memset(acc[:, :], 0.0).then_inc(sums_done, 1)

            def sums(n):
                clear(n)
                for d in range(KT - 1):
                    add_square(n, d)

            def residual(i):
                for d in range(0, KT, 2):
                    pool.wait_ge(u_ready, KT // 2 * i + d // 2 + 1)
                    pool.tensor_tensor(x[:, d, :], x[:, d, :], t[d % 2][:, :], ALU.add).then_inc(x_pool, 1)

            def rotate(stage):
                cs, sn, sh = (dcos, dsin, dshuf) if stage == "dsa" else (fcos, fsin, fshuf)
                n = ROT[stage]
                for j, kind in enumerate(DSA_KINDS if stage == "dsa" else DIFF_KINDS):
                    if kind == "rope":
                        q, s_ = rope_dst(stage, j), sh[j % 2][:, :]
                        pool.wait_ge(shuffled, n + 1)
                        pool.tensor_tensor(s_, s_, sn[:, :], ALU.mult)
                        pool.tensor_tensor(q, q, cs[:, :], ALU.mult).then_inc(rot_step, 1)
                        pool.wait_ge(rot_step, n + 1)
                        pool.tensor_tensor(q, q, s_, ALU.add).then_inc(rotated, 1)
                        n += 1

            def load_ada(n, parity):
                if not (isinstance(n, int) and n < 2):
                    pool.wait_ge(ada_used, n - 1)
                pool.dma_start(ada[parity][:, :], A["ada"][ds(n, 1)].rearrange("a p n -> (a p) n")).then_inc(
                    ada_landed[parity], 16)

            def load_static(stage):
                for j in range(dict(STAGE_UNITS)[stage]):
                    for n in ada_of(stage, j):
                        load_ada(n, n % 2)

            for stage in run:
                if stage == "in":
                    pool.wait_ge(b1_landed, 16 * 9)
                    pool.affine_select(out=ws[:, :, :], in_=ws[:, :, :], compare_op=ALU.is_ge, fill=0.0, base=0,
                                       pattern=[[0, 4], [1, P]], channel_multiplier=-1).then_inc(b1["ws"], 1)
                    load_static(stage)
                elif stage == "out":
                    with pool.Fori(0, 4) as it:
                        for u in range(len(FOX_MAPS)):
                            load_ada(ADA_FOX + u + len(FOX_MAPS) * it, (ADA_FOX + u) % 2)
                    clear(1)
                    load_ada(MOD_TILES - KT, 0)
                    for j in range(KT):
                        if j + 1 < KT:
                            load_ada(MOD_TILES - KT + j + 1, (j + 1) % 2)
                            add_square(1, j)
                elif stage.startswith("ffn"):
                    i = SUBS.index(stage)
                    for first, count, with_ada, part in loops(stage):
                        if part == "up" and with_ada:
                            with pool.Fori(0, count) as it:
                                for j in range(4):
                                    load_ada(ada_index(stage, first, j, it), (first + j) % 2)
                        elif part == "down":
                            def down(it):
                                for d in range(2):
                                    for j in (2 * d, 2 * d + 1):
                                        if with_ada:
                                            load_ada(ada_index(stage, first, j, it), (first + j) % 2)
                                    if not isinstance(it, int) or d == 0:
                                        add_square(POST[stage], d, 2 * it)
                            clear(POST[stage])
                            bodies(pool, count, down)
                    residual(i)
                elif stage == "dsa":
                    rotate(stage)
                elif stage == "diff":
                    rotate(stage)
                    pool.wait_ge(sub_inv, 1)
                    subln(pool, slice(3, 4))
                else:
                    sums(POST[stage[:-4]])
                    residual(SUBS.index(stage[:-4]))

        @block.vector
        def _(dve):
            chain = Chain(dve, dve_step)
            link = chain.link

            def lo(g, w, it=0):
                dve.wait_ge(hi_ready, g + 1 + 4 * it)
                dve.tensor_tensor(w_lo[g % N_SPLIT][:, 0:w], raw[g % N_RAW][:, 0:w],
                                  w_hi[g % N_SPLIT][:, 0:w].bitcast(F32), ALU.subtract).then_inc(lo_ready, 1)

            def lo_ahead(stage, j, it=0):
                g = UNIT_BASE[stage] + j + N_SPLIT
                if not isinstance(it, int):
                    lo(g, raw_width(stage, j), it)
                elif g + 4 * it < n_units:
                    lo(g, width_of(g + 4 * it), it)

            def mod_tile(n, parity, landed):
                dve.wait_ge(ada_landed[parity], landed)
                dve.scalar_tensor_tensor(out=ada[parity][:, :], in0=ada[parity][:, :], scalar=1.0, in1=cond[:, :],
                                         op0=ALU.mult, op1=ALU.mult,
                                         accum_out=mod_raw[:, ds(n, 1)]).then_inc(ada_used, 1)

            def mod_static(stage, j):
                for n in ada_of(stage, j):
                    mod_tile(n, n % 2, 16 * (n // 2 + 1))

            def mod_loop(stage, j, it):
                n = MOD_TILES + j + (0 if stage == "ffn0" else 2 * FT + 2 * KT)
                mod_tile(n + 4 * it, n % 2, 16 * (n // 2 + 1) + 32 * it)

            def finish_modulation(layer):
                dve.wait_ge(ada_used, MOD_TILES * (layer + 1))
                c0 = layer * MOD_TILES
                link(dve.tensor_tensor(mod_raw[:, c0:c0 + MOD_TILES], mod_raw[:, c0:c0 + MOD_TILES],
                                       cols[:, COL["ada_b"] + c0:COL["ada_b"] + c0 + MOD_TILES], ALU.add))
                for i in range(3 * layer, 3 * layer + 3):
                    at = c0 + 3 * (i % 3) * KT
                    c = slice(i * KT, (i + 1) * KT)
                    dve.scalar_tensor_tensor(out=gain[:, c], in0=mod_raw[:, at + KT:at + 2 * KT], scalar=1.0,
                                             in1=cols[:, COL["pre"] + i * KT:COL["pre"] + (i + 1) * KT],
                                             op0=ALU.add, op1=ALU.mult)
                    link(dve.scalar_tensor_tensor(out=coef[:, c], in0=mod_raw[:, at + 2 * KT:at + 3 * KT],
                                                  scalar=1.0 if i % 3 == 1 else 0.5,
                                                  in1=cols[:, COL["post"] + i * KT:COL["post"] + (i + 1) * KT],
                                                  op0=ALU.mult, op1=ALU.mult))

            def inverse(n):
                dve.wait_ge(sqrt_done, n + 1)
                dve.reciprocal(rstd[:, :], rstd[:, :]).then_inc(rstd_ready, 1)
                dve.wait_ge(rstd_ready, n + 1)

            def fill(stage, produce, tiles=range(KT), bias=None):
                tiles = list(tiles)
                for i in range(len(tiles) + 1):
                    if i < len(tiles):
                        if i >= 2:
                            dve.wait_ge(hl_ready, 8 * FILL[stage] + tiles[i - 2] + 1)
                        produce(tiles[i], t[tiles[i] % 2]).then_inc(t_ready, 1)
                    if i:
                        d = tiles[i - 1]
                        dve.wait_ge(hh_ready, 8 * FILL[stage] + d + 1)
                        dve.scalar_tensor_tensor(out=h_lo[:, d, :], in0=t[d % 2][:, :],
                                                 scalar=0.0 if bias is None else bias(d),
                                                 in1=h_hi[:, d, :].bitcast(F32), op0=ALU.add,
                                                 op1=ALU.subtract).then_inc(hl_ready, 1)

            def normed(gains, at):
                return lambda d, out_: dve.scalar_tensor_tensor(
                    out=out_[:, :], in0=x[:, d, :], scalar=gains[:, at + d:at + d + 1], in1=rstd[:, :],
                    op0=ALU.mult, op1=ALU.mult)

            def pre(stage):
                i = SUBS.index(stage)
                inverse(PRE[stage])
                fill(stage, normed(gain, i * KT), bias=lambda d: shift_col(i, d))

            def post(stage):
                i = SUBS.index(stage)
                inverse(POST[stage])
                for d in range(KT):
                    if d >= 2:
                        dve.wait_ge(*x_ready(i, d - 2))
                    ins = dve.scalar_tensor_tensor(out=t[d % 2][:, :], in0=y_of(stage)[:, d, :],
                                                   scalar=coef[:, i * KT + d:i * KT + d + 1], in1=rstd[:, :],
                                                   op0=ALU.mult, op1=ALU.mult)
                    if d % 2 == 0:
                        ins.then_inc(u_ready, 1)
                    else:
                        link(ins)
                        dve.tensor_tensor(x[:, d, :], x[:, d, :], t[1][:, :], ALU.add).then_inc(x_odd, 1)

            def ffn(stage):
                pre(stage)
                for first, count, with_ada, part in loops(stage):
                    def up(it):
                        for f in range(2):
                            j = first + 2 * f
                            lo_ahead(stage, j, it)
                            if with_ada:
                                mod_loop(stage, j, it)
                            lo_ahead(stage, j + 1, it)
                            if with_ada:
                                mod_loop(stage, j + 1, it)
                            fi = first // 2 + f + 2 * it
                            dve.wait_ge(*read_of(stage, j, it))
                            dve.wait_ge(unit_done, UNIT_BASE[stage] + j + 2 + 4 * it)
                            dve.tensor_tensor(t[f][:, :], sq[f][:, :], bank[2 * f + 1][:, :],
                                              ALU.mult).then_inc(bank_free[2 * f + 1], 1)
                            dve.wait_ge(ahi_ready, FT * ffn_no(stage) + fi + 1)
                            dve.tensor_tensor(a_lo[:, ds(fi, 1), :].rearrange("p a n -> p (a n)"), t[f][:, :],
                                              a_hi[:, ds(fi, 1), :].rearrange("p a n -> p (a n)").bitcast(F32),
                                              ALU.subtract).then_inc(alo_ready, 1)

                    def down(it):
                        for d in range(2):
                            j = first + 2 * d
                            lo_ahead(stage, j, it)
                            if with_ada:
                                mod_loop(stage, j, it)
                            lo_ahead(stage, j + 1, it)
                            if with_ada:
                                mod_loop(stage, j + 1, it)
                            dve.wait_ge(sq_ready, KT * POST[stage] + 2 * it + d + 1)
                            dve.tensor_copy(y[:, ds(2 * it + d, 1), :].rearrange("p a n -> p (a n)"),
                                            bank[d][:, :]).then_inc(bank_free[d], 1)
                    bodies(dve, count, up if part == "up" else down)
                post(stage)

            def projections(stage, kinds, on_tile):
                m, pending = TOK[stage], None

                def flush():
                    m_, j_ = pending
                    dve.wait_ge(tok_T, m_ + 1)
                    dve.tensor_copy(tok_dst(stage, j_), bank[4 + m_ % 2][:, :].rearrange("p (n c) -> p n c", n=NT)
                                    ).then_inc(tok_done, 1)
                for j, kind in enumerate(kinds):
                    lo_ahead(stage, j)
                    mod_static(stage, j)
                    if kind in ("copy", "tok"):
                        dve.wait_ge(unit_done, UNIT_BASE[stage] + j + 1)
                        if kind == "tok" and m - TOK[stage] >= 2:
                            dve.wait_ge(tok_T, m - 1)
                        dve.tensor_copy(sq[m % 2][:, :] if kind == "tok" else in_dst(j),
                                        bank[j % N_BANKS][:, :]).then_inc(bank_free[j % N_BANKS], 1)
                    elif kind == "rope":
                        on_tile(j)
                    if pending is not None:
                        flush()
                        pending = None
                    if kind.endswith("tok"):
                        pending = (m, j)
                        m += 1
                    if stage == "in":
                        beside_in(j)
                    elif stage == "dsa":
                        beside_dsa(j)
                if pending is not None:
                    flush()
                dve.wait_ge(tok_done, TOK_DONE[stage] + m - TOK[stage])

            def rope_tables(stage):
                r = rope[stage]
                cs, sn, sh = (dcos, dsin, dshuf) if stage == "dsa" else (fcos, fsin, fshuf)
                turn = 2 * np.pi
                c1 = 6.28125
                c2 = float(np.float32(int((turn - c1) * 2 ** 22) / 2 ** 22))
                c3 = float(turn - c1 - c2)
                magic = 1.5 * 2.0 ** 23
                dve.wait_ge(r["pos_landed"], 16)
                link(dve.tensor_copy(sh[1][:, :], sh[0][:, :].bitcast(I32)))
                link(dve.tensor_scalar(sh[1][:, :], sh[1][:, :], cols[:, COL["inv_freq"]:COL["inv_freq"] + 1], None, ALU.mult))
                link(dve.tensor_scalar(sh[0][:, :], sh[1][:, :], 1.0 / turn, magic, ALU.mult, ALU.add))
                link(dve.tensor_scalar(sh[0][:, :], sh[0][:, :], -magic, None, ALU.add))
                for c in (c1, c2, c3):
                    link(dve.scalar_tensor_tensor(out=sh[1][:, :], in0=sh[0][:, :], scalar=-c, in1=sh[1][:, :],
                                                  op0=ALU.mult, op1=ALU.add))
                below = float(np.nextafter(np.float32(np.pi), np.float32(0)))
                dve.tensor_scalar(sn[:, :], sh[1][:, :], below, -below, ALU.min, ALU.max).then_inc(r["angle"], 1)
                dve.wait_ge(r["angle"], 1)
                link(dve.scalar_tensor_tensor(out=cs[:, :], in0=sh[1][:, :], scalar=-1.0, in1=sh[1][:, :],
                                              op0=ALU.mult, op1=ALU.min))
                dve.tensor_scalar(cs[:, :], cs[:, :], float(np.pi / 2), None, ALU.add).then_inc(r["angle"], 1)
                dve.wait_ge(r["table"], 1)
                link(dve.tensor_scalar(sn[:, :], sn[:, :], cols[:, COL["sign"]:COL["sign"] + 1], None, ALU.mult))
                dve.wait_ge(r["table"], 2)

            def shuffle(stage, j):
                sh = dshuf if stage == "dsa" else fshuf
                n = ROT[stage] + j - (stage == "dsa")
                dve.wait_ge(*read_of(stage, j))
                if n >= ROT[stage] + 2:
                    dve.wait_ge(rotated, n - 1)
                swap = [(i + 8) % 16 if i < 16 else i for i in range(32)]
                dve.stream_shuffle(sh[j % 2][:, :], rope_dst(stage, j), swap).then_inc(shuffled, 1)

            def attend(k, cfg, maps, rounds):
                s = att[k]
                B = len(maps)
                s_t = cfg["st"]
                comps = 2 if k == "diff" else 1

                def queries(it):
                    for c in range(comps):
                        if k != "dsa":
                            dve.tensor_copy(cfg["ks"][:, c, :],
                                            cfg["k"][:, ds(it + 4 * c, 1), :].rearrange("p a n -> p (a n)"))
                        ins = dve.tensor_scalar(cfg["qs"][:, c, :],
                                                cfg["q"][:, ds(it + 4 * c, 1), :].rearrange("p a n -> p (a n)"),
                                                HD ** -0.5, None, ALU.mult)
                    ins.then_inc(s["qs_ready"], 1)

                def row_max(it, u):
                    w = (maps[u][2] + 1) * P
                    dve.wait_ge(s["s_ready"], B * it + u + 1)
                    dve.tensor_reduce(s_t[:, 0, u:u + 1], bank[u % 4][:, 0:w], AX, ALU.max,
                                      negate=True).then_inc(s["nm_ready"], 1)

                def output(it, u):
                    half, comp, qb = maps[u]
                    if k != "diff":
                        dve.wait_ge(s["o_ready"], B * it + u + 1)
                        link(dve.reciprocal(s_t[:, 2, u:u + 1], s_t[:, 1, u:u + 1]))
                        dve.tensor_scalar(cfg["otok"][:, qb, ds(it * P + half * HD, HD)], bank[6 + u % 2][:, 0:HD],
                                          s_t[:, 2, u:u + 1], None, ALU.mult).then_inc(s["o_read"], 1)
                    elif comp == 1:
                        dve.wait_ge(s["o_ready"], B * it + u + 1)
                        link(dve.reciprocal(s_t[:, 2, u - 1:u + 1], s_t[:, 1, u - 1:u + 1]))
                        link(dve.tensor_scalar(s_t[:, 2, u:u + 1], s_t[:, 2, u:u + 1], lam_col[:, 2:3], None, ALU.mult))
                        o_t, pair = cfg["ot"], bank[6 + u // 2 % 2]
                        link(dve.tensor_scalar(o_t[:, :], pair[:, P:2 * P], s_t[:, 2, u:u + 1], None, ALU.mult))
                        o = cfg["otok"][:, qb, ds(it * 2 * P + half * P, P)]
                        dve.scalar_tensor_tensor(out=o, in0=pair[:, 0:P], scalar=s_t[:, 2, u - 1:u], in1=o_t[:, :],
                                                 op0=ALU.mult, op1=ALU.subtract).then_inc(s["o_read"], 1)
                        dve.wait_ge(s["o_read"], 3 + B // 2 * it + u // 2)
                        link(dve.scalar_tensor_tensor(out=o_t[:, :], in0=o, scalar=1.0, in1=o, op0=ALU.mult,
                                                      op1=ALU.mult, accum_out=st_o[:, qb, ds(2 * it + half, 1)]))

                def body(it):
                    for u in range(B):
                        if u % 2:
                            w = (maps[u][2] + 1) * P
                            dve.wait_ge(s["tr_ready"], B * it + u + 1)
                            if u >= 2:
                                dve.wait_ge(s["o_ready"], B * it + u - 1)
                            dve.tensor_copy(cfg["PT"][:, 1, 0:w], bank[5][:, 0:w]).then_inc(s["pt_dve"], 1)
                        if u:
                            output(it, u - 1)
                        if later(maps, it, u + AHEAD):
                            row_max(*later(maps, it, u + AHEAD))
                        if u + AHEAD == B - 1 and not isinstance(it, int):
                            queries(it + 1)
                        if k == "fox":
                            n = ADA_FOX + u
                            mod_tile(n + B * it, n % 2, 16 * (n // 2 + 1) + 8 * B * it)
                    output(it, B - 1)

                for u in range(2):
                    dve.memset(s_t[:, 2, u:u + 1], 0.0).then_inc(s["o_read"], 1)
                queries(0)
                for u in range(AHEAD):
                    row_max(0, u)
                bodies(dve, rounds, body, chain, B // 2 * 4 if k == "diff" else B)
                dve.wait_ge(s["o_read"], 2 + (B // 2 if k == "diff" else B) * rounds)
                dve.tensor_copy(s_t[:, 2, 0:1], s_t[:, 1, 0:1]).then_inc(s["otok_done"], 1)

            rows3 = [P, NT, 256]
            groups = av[:, :, :].rearrange("p n (g c) -> p (n g) c", c=HD)
            bxg = bx[:, :, :].rearrange("p a (b c) -> p (a b) c", c=HD)

            def over(c):
                return st[:, c, :].unsqueeze(2).broadcast_to([P, 16, HD])

            def level_views(buf, m):
                v = buf[:, :, :].rearrange("p a (n s) -> p (a n) s", s=2 * m)
                return v[:, :, 0:m], v[:, :, m:2 * m], v[:, :, m - 1:m]

            def level_in(i):
                m = P >> (i + 1)
                dst = bf if i % 2 == 0 else bx
                low, high, _ = level_views(dst, m)
                b_low, b_high, mid = level_views(bb, m)
                mid = mid.broadcast_to([P, D // (2 * m), m])
                dve.tensor_tensor(low, mid, b_low, ALU.subtract)
                dve.tensor_tensor(high, b_high, mid, ALU.subtract).then_inc(b1["e_in"], 1)

            def level_out(i):
                m = P >> (i + 1)
                dst = bf if i % 2 == 0 else bx
                low, high, _ = level_views(dst, m)
                k_low, _, _ = level_views(bk, m)
                _, q_high, _ = level_views(bq, m)
                dve.wait_ge(b1["e_out"], 4 + i)
                dve.tensor_tensor(low, low, k_low, ALU.mult)
                dve.tensor_tensor(high, high, q_high, ALU.mult).then_inc(b1["x"], 1)

            def take(i):
                for h in range(4):
                    dve.wait_ge(b1["levels"], 4 * i + h + 1)
                    dve.copy_predicated(sc[:, h, :].rearrange("p (n s) -> p n s", n=NT),
                                        level[:, i, :].unsqueeze(1).broadcast_to([P, NT, P]),
                                        bank[h][:, :].rearrange("p (n s) -> p n s", n=NT)).then_inc(b1["copied"], 1)
            def beside_in(j):
                if j == 5:
                    dve.wait_ge(b1_landed, 16 * 9)
                    link(dve.tensor_copy(level[:, :, :], level_raw[:, :, :]))
                    lb = cols[:, COL["lb"]:COL["lb"] + 2]
                    dve.tensor_tensor(bcol[:, 0:2], lb, lb, ALU.subtract).then_inc(b1["lb"], 1)
                elif j == 6:
                    dve.wait_ge(tok_done, 2)
                    link(dve.tensor_reduce(st[:, 0, :], groups, AX, ALU.add))
                    link(dve.tensor_scalar(st[:, 1, :], st[:, 0, :], 1.0 / HD, None, ALU.mult))
                    link(dve.tensor_tensor(groups, groups, over(1), ALU.subtract))
                elif j == 7:
                    link(dve.tensor_tensor(bxg, groups, groups, ALU.mult))
                    dve.tensor_reduce(st[:, 2, :], bxg, AX, ALU.add).then_inc(b1["var"], 1)
                elif j == 9:
                    dve.wait_ge(b1["std"], 1)
                    link(dve.reciprocal(st[:, 3, :], st[:, 3, :]))
                    link(dve.tensor_tensor(groups, groups, over(3), ALU.mult))
                    link(dve.tensor_tensor(av[:, :, :], av[:, :, :], ln_g[:, :].unsqueeze(1).broadcast_to(rows3), ALU.mult))
                    dve.tensor_tensor(av[:, :, :], av[:, :, :], ln_b[:, :].unsqueeze(1).broadcast_to(rows3),
                                      ALU.add).then_inc(b1["vn"], 1)
                elif j == 11:
                    dve.wait_ge(b1["mixed"], 1)
                    dve.wait_ge(*read_of("in", 5))
                    dve.wait_ge(*read_of("in", 4))
                    for d in range(2):
                        u = bx[:, d, :]
                        link(dve.tensor_tensor(u.rearrange("p (n s) -> p n s", n=NT),
                                               bank[6 + d][:, :].rearrange("p (n s) -> p n s", n=NT),
                                               bs_bc[:, d, :].unsqueeze(1).broadcast_to([P, NT, P]), ALU.add))
                    link(dve.tensor_tensor(au[:, :, :], bx[:, :, :], au[:, :, :], ALU.mult))
                    link(dve.tensor_tensor(au[:, :, :], au[:, :, :], az[:, :, :], ALU.mult))
                elif j == 13:
                    dve.wait_ge(b1["lb_exp"], 1)
                    link(dve.reciprocal(bcol[:, 4:6], bcol[:, 2:4]))
                    link(dve.tensor_tensor(bcol[:, 2:4], bcol[:, 2:4], bcol[:, 4:6], ALU.mult))
                    link(dve.tensor_tensor(bcol[:, 4:6], bcol[:, 2:4], bcol[:, 2:4], ALU.subtract))
                    link(dve.tensor_scalar(bcol[:, 4:6], bcol[:, 4:6], 0.0, 1.0 - 1e-6, ALU.max, ALU.min))
                    link(dve.tensor_scalar(bcol[:, 6:8], bcol[:, 4:6], -1.0, 1.0, ALU.mult, ALU.add))
                    dve.wait_ge(b1["exps"], 2)
                    dve.tensor_scalar(bk[:, :, :], bk[:, :, :], 1.0, None, ALU.add)
                    link(dve.tensor_scalar(bt[:, :, :], bt[:, :, :], 1.0, None, ALU.add))
                elif j in (14, 15, 16, 17):
                    buf, a = (bk, bt)[j // 2 % 2 == 0], j % 2
                    link(dve.reciprocal(buf[:, a, :], buf[:, a, :]))
                elif j == 18:
                    for a in range(2):
                        dve.tensor_scalar(bk[:, a, :], bk[:, a, :], bcol[:, 6 + a:7 + a], None, ALU.mult)
                        link(dve.tensor_scalar(bt[:, a, :], bt[:, a, :], bcol[:, 6 + a:7 + a], bcol[:, 4 + a:5 + a],
                                               ALU.mult, ALU.add))
                    link(dve.tensor_scalar(bt[:, :, :], bt[:, :, :], F_FLOOR, None, ALU.max))
                elif j == 19:
                    link(dve.tensor_scalar(bx[:, :, :], bt[:, :, :], 2.0 ** -40, 2.0 ** 60, ALU.is_lt, ALU.mult))
                    link(dve.tensor_scalar(bx[:, :, :], bx[:, :, :], 1.0, None, ALU.max))
                elif j == 20:
                    dve.tensor_tensor(bf[:, :, :], bx[:, :, :], bt[:, :, :], ALU.mult).then_inc(b1["f"], 1)
                    dve.wait_ge(b1["f"], 1)
                    link(dve.tensor_scalar(bx[:, :, :], bt[:, :, :], 2.0 ** -40, float(-60 * np.log(2.0)),
                                           ALU.is_lt, ALU.mult))
                elif j == 23:
                    dve.wait_ge(b1["ln"], 1)
                    link(dve.tensor_tensor(bx[:, :, :], bx[:, :, :], bf[:, :, :], ALU.add))
                    for a in range(2):
                        ins = dve.tensor_tensor_scan(bb[:, a, :], keep, bx[:, a, :], 0.0, ALU.mult, ALU.add)
                        if a == 0:
                            link(ins)
                    ins.then_inc(b1["b"], 1)
                elif j == 24:
                    dve.wait_ge(*read_of("in", 7))
                    dve.wait_ge(*read_of("in", 6))
                    link(dve.tensor_scalar(bq[:, :, :], bq[:, :, :], HD ** -0.5, None, ALU.mult))
                    dve.wait_ge(b1["b"], 1)
                    chunks = bb[:, :, :].rearrange("p a (n s) -> p (a n) s", s=P)
                    dve.tensor_tensor(bx[:, :, :].rearrange("p a (n s) -> p (a n) s", s=P),
                                      chunks[:, :, P - 1:P].broadcast_to([P, 8, P]), chunks,
                                      ALU.subtract).then_inc(b1["e_in"], 1)
                elif j == 27:
                    dve.wait_ge(b1["e_out"], 2)
                    link(dve.tensor_tensor(bt[:, :, :], bt[:, :, :], bq[:, :, :], ALU.mult))
                    dve.wait_ge(b1["e_out"], 3)
                    dve.tensor_tensor(bx[:, :, :], bx[:, :, :], bk[:, :, :], ALU.mult).then_inc(b1["kh"], 1)
                elif j == 28:
                    level_in(0)
                elif j == 30:
                    for a in range(2):
                        dve.wait_ge(b1["kh_T"], a + 1)
                        dve.tensor_copy(kh_tok[:, :, a * P:(a + 1) * P],
                                        bank[4 + a][:, :].rearrange("p (n s) -> p n s", n=NT)).then_inc(b1["kh_tok"], 1)
                    level_in(1)

            def block1_mixers():
                fill("out", lambda d, out_: dve.tensor_copy(out_[:, :], au[:, d, :]), range(0, 2))
                dve.wait_ge(hl_ready, KT * FILL["out"] + 2)
                level_out(0)
                dve.memset(sc[:, :, :], 0.0).then_inc(b1["sc"], 1)

                s8, e8, ones8 = cf[0:8, :], t[0][0:8, :], t[1][0:8, :]
                link(dve.tensor_scalar(s8, s8, cols[0:8, COL["fox_b"]:COL["fox_b"] + 1], None, ALU.add))
                dve.scalar_tensor_tensor(out=e8, in0=s8, scalar=-1.0, in1=s8, op0=ALU.mult,
                                         op1=ALU.min).then_inc(b1["c_in"], 1)
                dve.wait_ge(b1["c_in"], 1)
                link(dve.tensor_scalar(s8, s8, 0.0, None, ALU.min))
                dve.wait_ge(b1["kv"], 1)
                kv = bank[6][:, 0:3 * 2 * HD].rearrange("p (n a c) -> p n a c", n=3, a=2)
                link(dve.tensor_copy(state[:, 0, :, :], kv[:, 0, :, :]))
                for n in (1, 2):
                    for a in range(2):
                        ins = dve.scalar_tensor_tensor(out=state[:, n, a, :], in0=state[:, n - 1, a, :],
                                                       scalar=bcol[:, 8 + 4 * a + n:9 + 4 * a + n], in1=kv[:, n, a, :],
                                                       op0=ALU.mult, op1=ALU.add)
                        if (n, a) != (2, 1):
                            link(ins)
                ins.then_inc(b1["state"], 1)
                dve.wait_ge(b1["sc"], 1)
                for i in range(7):
                    if i + 1 < 7:
                        level_out(i + 1)
                    take(i)
                    if i + 2 < 7:
                        level_in(i + 2)
                    if i == 0:
                        dve.wait_ge(b1["c_out"], 1)
                        dve.memset(ones8, 1.0)
                        dve.tensor_scalar(e8, e8, 1.0, None, ALU.add).then_inc(b1["c_in"], 1)
                    elif i == 2:
                        dve.wait_ge(b1["c_out"], 2)
                        link(dve.tensor_tensor(e8, e8, s8, ALU.subtract))
                        dve.tensor_tensor_scan(s8, ones8, e8, 0.0, ALU.mult, ALU.add).then_inc(fox_c_ready, 1)
                take(7)
                link(dve.memset(ws[:, 0, :], 0.0))
                dve.memset(ws[0:HD, 0, 0:HD], 1.0)
                link(dve.memset(ws[HD:P, 0, HD:P], 1.0))
                dve.tensor_copy(bcol[:, 63:64], bcol[:, 8:9]).then_inc(b1["bd"], 1)
                for a in range(2):
                    dve.wait_ge(b1["ostd"], a + 1)
                    link(dve.reciprocal(bt[:, a, :], bt[:, a, :]))

                def hgrn_out(d, out_):
                    a = d - 2
                    link(dve.scalar_tensor_tensor(out=bx[:, a, :], in0=bank[4 + a][:, :],
                                                  scalar=cols[:, COL["onorm"]:COL["onorm"] + 1], in1=bt[:, a, :],
                                                  op0=ALU.mult, op1=ALU.mult))
                    return dve.tensor_tensor(out_[:, :], bx[:, a, :], bz[:, a, :], ALU.mult)
                fill("out", hgrn_out, range(2, 4))

                attend("fox", block1, FOX_MAPS, 4)

                def fox_out(d, out_):
                    m = TOK["fox_out"] + d - 4
                    dve.wait_ge(tok_T, m + 1)
                    return dve.tensor_tensor(out_[:, :], bank[4 + m % 2][:, :], cz[:, d - 4, :], ALU.mult)
                fill("out", fox_out, range(4, 8))

            def beside_dsa(j):
                if j == 6:
                    link(dve.tensor_scalar(wi[:, :, :], dv[:, :, HD:HD + 8], float(8 ** -0.5 * HD ** -0.5), None, ALU.mult))
                    link(dve.tensor_copy(mask[:, 0, 0:P], causal_bf[:, :]))
                if j not in TOP_AT:
                    return
                qb, first, end = TOP_AT[j]
                w = (qb + 1) * P
                s_ = [b[:, 0:w] for b in score]
                if j == IX_AT[qb]:
                    for h in range(8):
                        n = 8 * (qb - 1) + h
                        dve.wait_ge(ix["relu"], n + 1)
                        r_ = rel[n % 2][:, 0:w]
                        if h == 0:
                            ins = dve.tensor_scalar(s_[0], r_, wi[:, qb, 0:1], None, ALU.mult)
                        else:
                            ins = dve.scalar_tensor_tensor(out=s_[0], in0=r_, scalar=wi[:, qb, h:h + 1], in1=s_[0],
                                                           op0=ALU.mult, op1=ALU.add)
                        ins.then_inc(ix["read"], 1)
                        dve.wait_ge(ix["read"], n + 1)
                    link(dve.tensor_tensor(score[0][:, qb * P:w], score[0][:, qb * P:w], causal_bf[:, :], ALU.add))
                for r in range(first, end):
                    link(dve.max(top8[:, 0, :], s_[r % 2]))
                    link(dve.match_replace(s_[(r + 1) % 2], top8[:, 0, :], s_[r % 2], TAKEN))
                if end == TOPK // 8:
                    ins = dve.tensor_scalar(mask[:, qb, 0:w], s_[0], TAKEN / 1.5, NEG, ALU.is_ge, ALU.mult)
                    if qb < NT - 1:
                        link(ins)
                    else:
                        ins.then_inc(ix["mask"], 1)

            def turned(stage, scale=None):
                def produce(d, out_):
                    m = TOK[stage] + d
                    dve.wait_ge(tok_T, m + 1)
                    if scale is None:
                        return dve.tensor_copy(out_[:, :], bank[4 + m % 2][:, :])
                    return dve.tensor_scalar(out_[:, :], bank[4 + m % 2][:, :], scale, 1.0 - LAM_INIT,
                                             ALU.mult, ALU.mult)
                return produce

            dve.memset(eps_col[:, :], EPS)
            dve.memset(ones[:, :], 1.0).then_inc(ones_ready, 1)
            dve.wait_ge(const_landed, 48)
            dve.tensor_copy(ident_bf[:, :], ident[:, :])
            dve.tensor_copy(causal_bf[:, :], t[0][:, 0:P]).then_inc(const_ready, 1)
            dve.wait_ge(const_ready, 1)
            for g in range(N_SPLIT):
                lo(g, D)
            for stage in run:
                if stage == "in":
                    inverse(0)
                    fill(stage, normed(cols, COL["norm_g"]))
                    dve.wait_ge(cond_ready, 1)
                    projections(stage, IN_KINDS, None)
                elif stage == "out":
                    block1_mixers()
                    for j in range(KT):
                        lo_ahead(stage, j)
                        mod_static(stage, j)
                        dve.wait_ge(unit_done, UNIT_BASE[stage] + j + 1)
                        dve.tensor_tensor(x[:, j, :], x[:, j, :], bank[j % N_BANKS][:, :],
                                          ALU.add).then_inc(bank_free[j % N_BANKS], 1)
                    finish_modulation(0)
                    inverse(1)
                    for j in range(KT - N_BANKS, KT):
                        dve.wait_ge(*read_of(stage, j))
                    for d in range(KT):
                        normed(cols, COL["final_g"])(d, x[:, d, :]).then_inc(x_dve, 1)
                elif stage.startswith("ffn"):
                    if stage == "ffn2":
                        finish_modulation(1)
                    ffn(stage)
                elif stage in ("dsa", "diff"):
                    pre(stage)
                    rope_tables(stage)
                    projections(stage, DSA_KINDS if stage == "dsa" else DIFF_KINDS, lambda j: shuffle(stage, j))
                    dve.wait_ge(rotated, ROT[stage] + (14 if stage == "dsa" else 16))
                    if stage == "dsa":
                        attend("dsa", dsa, DSA_MAPS, 8)
                    else:
                        dve.wait_ge(lam_landed, 16)
                        for c in range(2):
                            link(dve.tensor_tensor(lam_in[:, 2 * c, :], lam_in[:, 2 * c, :], lam_in[:, 2 * c + 1, :], ALU.mult))
                            ins = dve.tensor_reduce(lam_col[:, c:c + 1], lam_in[:, 2 * c, :], AX, ALU.add)
                        ins.then_inc(lam_sum, 1)
                        dve.wait_ge(lam_exp, 1)
                        link(dve.scalar_tensor_tensor(out=lam_col[:, 2:3], in0=lam_col[:, 0:1], scalar=LAM_INIT,
                                                      in1=lam_col[:, 1:2], op0=ALU.add, op1=ALU.subtract))
                        attend("diff", diff, DIFF_MAPS, 4)
                        dve.wait_ge(sub_std, 1)
                        dve.reciprocal(st_o[:, :, :], st_o[:, :, :]).then_inc(sub_inv, 1)
                        dve.wait_ge(sub_inv, 1)
                        subln(dve, slice(0, 3))
                else:
                    sub = stage[:-4]
                    fill(stage, turned(stage, None if sub == "dsa" else cols[:, COL["subln"]:COL["subln"] + 1]))
                    for j in range(KT):
                        lo_ahead(stage, j)
                        dve.wait_ge(unit_done, UNIT_BASE[stage] + j + 1)
                        dve.tensor_copy(y_mix[:, j, :], bank[j % N_BANKS][:, :]).then_inc(bank_free[j % N_BANKS], 1)
                    post(sub)


def units_of(w):
    k, n = w.shape
    return np.ascontiguousarray(w.reshape(k // P, P, n // P, P).transpose(2, 1, 0, 3).reshape(n // P, P, k))


def columns(v):
    return np.ascontiguousarray(v.reshape(-1, P).T)


def lay_out(i):
    f32 = np.float32
    w_in = i["w_in"][0]
    w_in = np.concatenate([w_in, np.zeros((D, len(IN_KINDS) * P - w_in.shape[1]), f32)], axis=1)
    up, down = [], []
    for layer in range(N_LAYERS):
        for s in range(2):
            pad = np.zeros((D, FT * P - F_FF), f32)
            g = units_of(np.concatenate([i["ffn_w_gate_2"][layer, s], pad], axis=1))
            u = units_of(np.concatenate([i["ffn_w_up_2"][layer, s], pad], axis=1))
            up.append(np.stack([g, u], axis=1).reshape(2 * FT, P, D))
            dn = units_of(np.concatenate([i["ffn_w_down_2"][layer, s], pad.T], axis=0))
            down.append(dn.reshape(KT, P, 2, FH * P).transpose(0, 2, 1, 3).reshape(2 * KT, P, FH * P))
    w = i["dsa_w_in_2"][0]
    q, k, v, qi, ki, wi_ = np.split(w, np.cumsum([16 * HD, HD, HD, 8 * HD, HD]), axis=1)
    w_dsa = np.concatenate([v, wi_, np.zeros((D, P - HD - 8), f32), qi, ki, ki, k, k, q], axis=1)
    inv = np.zeros(P, f32)
    sign = np.zeros(P, f32)
    rot = HD // ROT_FRAC
    freq = (ROPE_THETA ** (-np.arange(0, rot, 2, dtype=f32) / rot)).astype(f32)
    for p in range(P):
        if p % HD < rot:
            inv[p] = freq[p % HD % (rot // 2)]
            sign[p] = -1.0 if p % HD < rot // 2 else 1.0
    fox_b = np.zeros((P, 1), f32)
    fox_b[0:8, 0] = i["fox_b_f"][0]
    cols = np.concatenate([
        columns(i["norm_g"][0]), columns(i["final_norm_g"]), columns(i["pre_norm_2"]), columns(i["post_norm_2"]),
        columns(i["ada_b_2"]), np.tile(i["hgrn_onorm_g"][0], 2)[:, None], i["diff_subln_2"][0][:, None],
        columns(i["hgrn_lb"][0]), inv[:, None], sign[:, None], fox_b], axis=1).astype(f32)
    assert cols.shape == (P, N_COLS)
    key, query = np.arange(P)[:, None], np.arange(P)[None, :]
    level = np.zeros((P, 8, P), f32)
    for n in range(7):
        m = P >> (n + 1)
        level[:, n, :] = (key // (2 * m) == query // (2 * m)) & (key % (2 * m) < m) & (query % (2 * m) >= m)
    level[:, 7, :] = key == query
    keep = np.ones((P, SEQ), f32)
    keep[:, ::P] = 0.0
    return {
        "x": np.ascontiguousarray(i["x"][0].T), "cols": cols, "ident": np.eye(P, dtype=f32),
        "causal": np.where(query <= key, 0.0, NEG).astype(f32), "c": i["c_2"][0], "pos": i["positions_2"][0],
        "ws": np.ascontiguousarray(i["gmlp_w_s"][0].transpose(2, 0, 1)), "level": level, "keep": keep,
        "ln_g": i["gmlp_ln_g"][0].reshape(-1), "ln_b": i["gmlp_ln_b"][0].reshape(-1), "bs": i["gmlp_b_s"][0],
        "lam": i["diff_lambda_2"][0].reshape(-1),
        "ada": np.ascontiguousarray(i["ada_w_2"].transpose(0, 2, 1).reshape(2 * MOD_TILES, P, D)),
        "w_in": units_of(w_in), "w_out": units_of(i["w_out"][0]),
        "ffn_up": np.stack(up), "ffn_down": np.stack(down),
        "w_dsa": units_of(w_dsa), "w_dsa_out": units_of(i["dsa_w_out_2"][0]),
        "w_diff": units_of(i["diff_w_in_2"][0]), "w_diff_out": units_of(i["diff_w_out_2"][0]),
    }


def kernel(**inputs):
    import concourse.bacc as bacc
    from concourse.bass_utils import run_bass_kernel_spmd

    arrays = {f"in_{k}": np.ascontiguousarray(v) for k, v in lay_out({k: np.asarray(v) for k, v in inputs.items()}).items()}
    nc = bacc.Bacc("TRN2", target_bir_lowering=False, num_devices=1)
    A = {k[3:]: nc.dram_tensor(k, v.shape, mybir.dt.from_np(v.dtype), kind="ExternalInput").ap()
         for k, v in arrays.items()}
    out = nc.dram_tensor("out_0", (D, SEQ), F32, kind="ExternalOutput").ap()
    build(nc, A, out)
    r = run_bass_kernel_spmd(nc, [arrays], core_ids=[0])
    return np.ascontiguousarray(r.results[0]["out_0"].T)[None]
```
